# Optimizing a Trainium2 kernel written in Bass

```python
import jax, jax.numpy as jnp
from jax import lax
import numpy as np

D_MODEL = 1024
BATCH = 1
SEQ = 1024
DEPTH = 1
DEC_BATCH = 8
DEC_SEQ = 16
PAST_LEN = 1024

CHUNK = 64
D_MIX = D_MODEL
D_ATTN = D_MIX // 2
D_POOL = D_MIX - D_ATTN
HEAD_DIM = 64
N_Q_HEADS = D_ATTN // HEAD_DIM
N_KV_HEADS = 2
Q_PER_KV = N_Q_HEADS // N_KV_HEADS
D_KV = N_KV_HEADS * HEAD_DIM
WINDOW = 128
WIN_CHUNKS = WINDOW // CHUNK
ROPE_THETA = 10000.0
POOL_WINDOWS = (2, 4, 8, 16)
N_POOL_GROUPS = len(POOL_WINDOWS)
POOL_GROUP = D_POOL // N_POOL_GROUPS
POOL_HIST = max(POOL_WINDOWS) - 1
D_IN = D_ATTN + 2 * D_KV + D_ATTN + D_POOL + D_POOL
LN_EPS = 1e-5
DN_ALPHA = (2 * DEPTH) ** 0.25
DN_BETA = (8 * DEPTH) ** -0.25
NEG_INF = -1e30

kernel_name = "hybrid_swa_sink_pool_streaming_step"

def _layer_norm(x):
    xf = x.astype(jnp.float32)
    mu = jnp.mean(xf, axis=-1, keepdims=True)
    var = jnp.mean(jnp.square(xf - mu), axis=-1, keepdims=True)
    return (xf - mu) * lax.rsqrt(var + LN_EPS)

def _rope(t, pos):
    half = HEAD_DIM // 2
    inv = ROPE_THETA ** (-jnp.arange(half, dtype=jnp.float32) / half)
    ang = pos.astype(jnp.float32)[:, None] * inv[None, :]
    cos = jnp.cos(ang)[None, :, None, :]
    sin = jnp.sin(ang)[None, :, None, :]
    tf = t.astype(jnp.float32)
    t1, t2 = tf[..., :half], tf[..., half:]
    return jnp.concatenate([t1 * cos - t2 * sin, t2 * cos + t1 * sin], axis=-1).astype(t.dtype)

def _front(x, c, pos, w_ada, b_ada, w_in):
    B, L, _ = x.shape
    mod = jax.nn.silu(c) @ w_ada + b_ada
    shift, scale, gate = jnp.split(mod, 3, axis=-1)
    h = (_layer_norm(x) * (1.0 + scale[:, None, :].astype(jnp.float32))
         + shift[:, None, :].astype(jnp.float32)).astype(x.dtype)
    proj = h @ w_in
    cuts = np.cumsum([D_ATTN, D_KV, D_KV, D_ATTN, D_POOL])
    q, k, v, g_attn, u, g_pool = jnp.split(proj, cuts, axis=-1)
    q = _rope(q.reshape(B, L, N_Q_HEADS, HEAD_DIM), pos)
    k = _rope(k.reshape(B, L, N_KV_HEADS, HEAD_DIM), pos)
    v = v.reshape(B, L, N_KV_HEADS, HEAD_DIM)
    return q, k, v, g_attn, u, g_pool, gate

def _sink_attention(q, k, v, q_pos, k_pos, sinks):
    B, N, Lq = q.shape[:3]
    qg = q.reshape(B, N, Lq, N_KV_HEADS, Q_PER_KV, HEAD_DIM)
    s = jnp.einsum('bnqhgd,bnkhd->bnhgqk', qg, k).astype(jnp.float32) * (HEAD_DIM ** -0.5)
    dc = (q_pos // CHUNK)[:, :, None] - (k_pos // CHUNK)[:, None, :]
    mask = (k_pos[:, None, :] >= 0) & (dc >= 0) & (dc <= WIN_CHUNKS)
    s = jnp.where(mask[None, :, None, None], s, NEG_INF)
    sk = sinks.astype(jnp.float32).reshape(N_KV_HEADS, Q_PER_KV)[None, None, :, :, None, None]
    m = jnp.maximum(jnp.max(s, axis=-1, keepdims=True), sk)
    p = jnp.exp(s - m)
    p = (p / (jnp.sum(p, axis=-1, keepdims=True) + jnp.exp(sk - m))).astype(v.dtype)
    o = jnp.einsum('bnhgqk,bnkhd->bnqhgd', p, v)
    return o.reshape(B, N, Lq, D_ATTN)

def _attn_prompt(q, k, v, sinks):
    B, T = q.shape[:2]
    n_c = T // CHUNK
    qb = q.reshape(B, n_c, CHUNK, N_Q_HEADS, HEAD_DIM)

    def band(t):
        tb = t.reshape(B, n_c, CHUNK, N_KV_HEADS, HEAD_DIM)
        tp = jnp.pad(tb, ((0, 0), (WIN_CHUNKS, 0), (0, 0), (0, 0), (0, 0)))
        return jnp.concatenate([tp[:, j:j + n_c] for j in range(WIN_CHUNKS + 1)], axis=2)

    kp = jnp.arange(-WIN_CHUNKS * CHUNK, T, dtype=jnp.int32).reshape(n_c + WIN_CHUNKS, CHUNK)
    k_pos = jnp.concatenate([kp[j:j + n_c] for j in range(WIN_CHUNKS + 1)], axis=1)
    q_pos = jnp.arange(T, dtype=jnp.int32).reshape(n_c, CHUNK)
    o = _sink_attention(qb, band(k), band(v), q_pos, k_pos, sinks)
    return o.reshape(B, T, D_ATTN)

def _attn_sample(q, k_all, v_all, q_pos, k_pos, sinks):
    o = _sink_attention(q[:, None], k_all[:, None], v_all[:, None], q_pos[None], k_pos[None], sinks)
    return o[:, 0]

def _pool_mix(u, hist, pos0, w_pool, pool_scale):
    B, L, _ = u.shape
    P = hist.shape[1]
    ue = jnp.concatenate([hist, u], axis=1).astype(jnp.float32)
    cs = jnp.pad(jnp.cumsum(ue, axis=1), ((0, 0), (1, 0), (0, 0)))
    pos = pos0 + jnp.arange(L, dtype=jnp.int32)
    outs = []
    for g, w in enumerate(POOL_WINDOWS):
        sl = slice(g * POOL_GROUP, (g + 1) * POOL_GROUP)
        s = cs[:, P + 1:P + 1 + L, sl] - cs[:, P + 1 - w:P + 1 - w + L, sl]
        cnt = jnp.minimum(pos + 1, w).astype(jnp.float32)
        outs.append(s / cnt[None, :, None])
    d = (jnp.concatenate(outs, axis=-1) - u.astype(jnp.float32)).reshape(B, L, N_POOL_GROUPS, POOL_GROUP)
    z = jnp.einsum('blgc,gcd->blgd', d, w_pool.astype(jnp.float32)).reshape(B, L, D_POOL)
    return (z * pool_scale.astype(jnp.float32)).astype(u.dtype)

def _back(x, o_attn, g_attn, o_pool, g_pool, gate, w_out, ln_g, ln_b):
    mixed = jnp.concatenate([o_attn * jax.nn.silu(g_attn), o_pool * jax.nn.silu(g_pool)], axis=-1)
    y = mixed @ w_out
    r = DN_ALPHA * x + gate[:, None, :] * y
    return (_layer_norm(r) * ln_g.astype(jnp.float32) + ln_b.astype(jnp.float32)).astype(x.dtype)

def setup_inputs(seed: int = 0) -> dict:
    key = jax.random.key(seed)
    ks = jax.random.split(key, 16)
    f32 = jnp.float32
    rows = min(WINDOW, PAST_LEN)
    nrm = lambda k, s, sc: jax.random.normal(k, s, f32) * sc
    w_in = nrm(ks[7], (DEPTH, D_MODEL, D_IN), D_MODEL ** -0.5)
    v0 = D_ATTN + D_KV
    w_in = w_in.at[:, :, v0:v0 + D_KV].multiply(DN_BETA)
    return {
        "x_prompt": nrm(ks[0], (BATCH, SEQ, D_MODEL), 1.0),
        "x_sample": nrm(ks[1], (DEC_BATCH, DEC_SEQ, D_MODEL), 1.0),
        "cache_k": nrm(ks[2], (DEPTH, DEC_BATCH, rows, N_KV_HEADS, HEAD_DIM), 1.0),
        "cache_v": nrm(ks[3], (DEPTH, DEC_BATCH, rows, N_KV_HEADS, HEAD_DIM), DN_BETA),
        "state_pool": nrm(ks[4], (DEPTH, DEC_BATCH, POOL_HIST, D_POOL), 1.0),
        "c_prompt": nrm(ks[5], (BATCH, D_MODEL), 1.0),
        "c_sample": nrm(ks[6], (DEC_BATCH, D_MODEL), 1.0),
        "w_ada": nrm(ks[8], (DEPTH, D_MODEL, 3 * D_MODEL), 0.5 * D_MODEL ** -0.5),
        "b_ada": nrm(ks[9], (DEPTH, 3 * D_MODEL), 0.02),
        "w_in": w_in,
        "attn_sinks": nrm(ks[10], (DEPTH, N_Q_HEADS), 0.5),
        "w_pool": nrm(ks[11], (DEPTH, N_POOL_GROUPS, POOL_GROUP, POOL_GROUP), POOL_GROUP ** -0.5),
        "pool_scale": 1.0 + nrm(ks[12], (DEPTH, D_POOL), 0.1),
        "w_out": nrm(ks[13], (DEPTH, D_MIX, D_MODEL), DN_BETA * D_MIX ** -0.5),
        "ln_g": 1.0 + nrm(ks[14], (DEPTH, D_MODEL), 0.05),
        "ln_b": nrm(ks[15], (DEPTH, D_MODEL), 0.02),
    }

def reference(x_prompt, x_sample, cache_k, cache_v, state_pool, c_prompt, c_sample,
              w_ada, b_ada, w_in, attn_sinks, w_pool, pool_scale, w_out, ln_g, ln_b):
    T = x_prompt.shape[1]
    L = x_sample.shape[1]
    rows = cache_k.shape[2]
    pos_p = jnp.arange(T, dtype=jnp.int32)
    pos_s = PAST_LEN + jnp.arange(L, dtype=jnp.int32)
    k_pos_s = jnp.concatenate([jnp.arange(PAST_LEN - rows, PAST_LEN, dtype=jnp.int32), pos_s])
    yp, ys = x_prompt, x_sample
    nkp, nvp, nup, nks, nvs, nus = [], [], [], [], [], []
    for l in range(DEPTH):
        q, k, v, ga, u, gp, gate = _front(yp, c_prompt, pos_p, w_ada[l], b_ada[l], w_in[l])
        o_a = _attn_prompt(q, k, v, attn_sinks[l])
        hist0 = jnp.zeros((yp.shape[0], POOL_HIST, D_POOL), u.dtype)
        o_p = _pool_mix(u, hist0, 0, w_pool[l], pool_scale[l])
        yp = _back(yp, o_a, ga, o_p, gp, gate, w_out[l], ln_g[l], ln_b[l])
        nkp.append(k[:, -WINDOW:])
        nvp.append(v[:, -WINDOW:])
        nup.append(u[:, -POOL_HIST:])
        q, k, v, ga, u, gp, gate = _front(ys, c_sample, pos_s, w_ada[l], b_ada[l], w_in[l])
        k_all = jnp.concatenate([cache_k[l].astype(k.dtype), k], axis=1)
        v_all = jnp.concatenate([cache_v[l].astype(v.dtype), v], axis=1)
        o_a = _attn_sample(q, k_all, v_all, pos_s, k_pos_s, attn_sinks[l])
        hist = state_pool[l].astype(u.dtype)
        o_p = _pool_mix(u, hist, PAST_LEN, w_pool[l], pool_scale[l])
        ys = _back(ys, o_a, ga, o_p, gp, gate, w_out[l], ln_g[l], ln_b[l])
        nks.append(k_all[:, -rows:])
        nvs.append(v_all[:, -rows:])
        nus.append(jnp.concatenate([hist, u], axis=1)[:, -POOL_HIST:])
    return (yp, ys, jnp.stack(nkp), jnp.stack(nvp), jnp.stack(nup),
            jnp.stack(nks), jnp.stack(nvs), jnp.stack(nus))


_drawn_inputs = setup_inputs


def setup_inputs(seed=0):
    import zlib

    import numpy as np

    out = dict(_drawn_inputs(seed))
    spreads = {}
    factors = {'state_pool': 5.01, 'attn_sinks': 8.0, 'pool_scale': 8.0, 'ln_b': 2.869}
    for name, (base, spread) in spreads.items():
        noise = np.random.default_rng([zlib.crc32(name.encode()), seed]).standard_normal(out[name].shape)
        drawn = base * np.exp(spread * noise) if base else spread * noise
        out[name] = __import__('jax').numpy.asarray(drawn.astype(out[name].dtype))
    for name, factor in factors.items():
        out[name] = (out[name] * factor).astype(out[name].dtype)
    return out
```

```python
import concourse.bass as bass
from concourse import mybir
import numpy as np

F32 = mybir.dt.float32
F32R = mybir.dt.float32r
ALU = mybir.AluOpType
ACT = mybir.ActivationFunctionType
AX = mybir.AxisListType

P = 128
D = 1024
SEQ = 1024
NSEQ = 8
LS = 16
TOK = SEQ + NSEQ * LS
KT = D // P
TILES = TOK // P
NCH = 3
CW = TOK // NCH
PW2 = SEQ - 2 * CW
HD = 64
QB = 64
NQ = 16
WIN = 128
HIST = 15
NSP = NSEQ // 2
NSTEP = NQ + NSP
ALPHA = float(2.0 ** 0.25)
EPS = 1e-5
SCALE = HD ** -0.5
UE = HIST + SEQ
UW = UE + NSEQ * (HIST + LS)
UB = (UW + 7) // 8 * 8

ADA = [0, 2, 1, 3, 4, 5]

K_BLK, V_BLK = 0, 1
GA_BLK = [2, 3, 4, 5]
Q_BLK = [6, 7, 8, 9]
U_BLK = [10, 12, 14, 16]
GP_BLK = [11, 13, 15, 17]
NBLK = 18


def unit_list():
    units = []
    for c in range(NCH):
        units += [("k", 0, c), ("v", 0, c)]
    units += [("ga", j, c) for j in range(4) for c in range(NCH)]
    units += [("q", j, c) for j in range(4) for c in range(NCH)]
    for g in range(4):
        units += [("u", g, c) for c in range(NCH)]
        units += [("gp", g, c) for c in range(NCH)]
        units += [("z", g, c) for c in range(NCH)]
    units += [("r", row, half) for row in range(2) for half in range(2)]
    return units


UNITS = unit_list()
NU = len(UNITS)
BLOCK_OF = {"k": [K_BLK], "v": [V_BLK], "ga": GA_BLK, "q": Q_BLK, "u": U_BLK, "gp": GP_BLK}


def block_of(n):
    kind, j, _ = UNITS[n]
    return BLOCK_OF[kind][j] if kind in BLOCK_OF else None


LAST_UNIT = {block_of(n): n for n in range(NU) if block_of(n) is not None}
FIRST_UNIT = {block_of(n): n for n in reversed(range(NU)) if block_of(n) is not None}
LAST_PROJ = max(LAST_UNIT.values())
FREED_BY_ACT = ("v", "u", "r")


def freed_count(n):
    act = UNITS[n][0] in FREED_BY_ACT
    return act, sum((UNITS[m][0] in FREED_BY_ACT) == act for m in range(n + 1))


def count(kinds, n):
    return sum(UNITS[m][0] in kinds for m in range(n + 1))


def unit_index(kind, j, c):
    return UNITS.index((kind, j, c))


GATES = [n for n in range(NU) if UNITS[n][0] in ("ga", "gp")]

SLOT0 = 29
SLOTS = {}
for _s in range(NSTEP + 2):
    SLOTS.setdefault(min(SLOT0 + 2 * _s, SLOT0 + 22 + _s, NU - 1), []).append(_s)


def keys_of(i):
    if i >= NQ:
        return WIN, LS
    nk = min(i + 1, 3) * QB
    return min(nk, WIN), max(nk - WIN, 0)


def seconds(i):
    return sum(keys_of(s)[1] > 0 for s in range(i + 1))


def hybrid_step(nc, x_all, cT_d, bT_d, w_ada, w_in, w_out, w_pool, pscale_d, sinkp_d, sinks_d, kcT, vc, kc_tail, vc_tail,
                histT, ln_g, ln_b, ident_d, sel_d, ebc_d, brow_d, cos_d, sin_d,
                y_out, kT_out, vT_out, upT_out, usT_out, kcT_out, vc_out):
    top = [nc.sbuf_base + 31 & ~31]

    def place(name, shape, dt=F32, at=None):
        size = 4
        for s in shape[1:]:
            size *= s
        if at is None:
            at = top[0]
            top[0] = (at + size + 31) & ~31
        return nc.alloc_sbuf_tensor_at(name, shape, dt, offset=at)

    def region(size):
        at = top[0]
        top[0] = (at + size + 31) & ~31
        return at

    r_h = region(2 * KT * TOK * 4)
    h_hi = place("h_hi", [P, KT, TOK], F32R, at=r_h)
    h_lo = place("h_lo", [P, KT, TOK], F32R, at=r_h + KT * TOK * 4)
    wo_hi = place("wo_hi", [P, KT, D], F32R, at=r_h)
    wo_lo = place("wo_lo", [P, KT, D], F32R, at=r_h + KT * TOK * 4)
    r_mx = region(KT * TOK * 4)
    xnT = place("xnT", [P, KT, TOK], at=r_mx)
    mixed = place("mixed", [P, KT, TOK], at=r_mx)
    r_q = region(4 * TOK * 4)
    qP = place("qP", [P, NQ, 4, QB], at=r_q)
    qS = place("qS", [P, NSEQ, 4, LS], at=r_q + NQ * 4 * QB * 4)
    xs = place("xs", [P, 4, D], at=r_q)
    wada_late = place("wada_late", [P, KT, 512], at=r_q)
    r_a = top[0]
    Vc = place("Vc", [P, NQ, P])
    r_p = top[0]
    Pb = place("Pb", [P, 2, 4, 192])
    PT1 = place("PT1", [P, 512])
    PT2 = place("PT2", [P, 512])
    vT = place("vT", [P, TOK], at=r_p)
    r_k = top[0]
    kT = place("kT", [P, TOK])
    th = place("th", [P, 2, CW])
    Ks = place("Ks", [P, 2, 2, WIN])
    Vs = place("Vs", [P, 2, 2, P])
    r_u = region(3 * UB * 4)
    rt1 = place("rt1", [P, 2, CW], at=r_u)
    rt2 = place("rt2", [P, 2, CW], at=r_u + 2 * CW * 4)
    cosT = place("cosT", [P, TOK], at=r_u + 4 * CW * 4)
    sinT = place("sinT", [P, TOK], at=r_u + 4 * CW * 4 + TOK * 4)
    assert 4 * CW * 4 + 2 * TOK * 4 <= 3 * UB * 4
    uext = place("uext", [P, UW], at=r_u)
    sA = place("sA", [P, UW], at=r_u + UB * 4)
    sB = place("sB", [P, UW], at=r_u + 2 * UB * 4)
    wada = [place(f"wada{s}", [P, KT, 512], at=r_a + 16384 * s) for s in range(2)]
    assert r_a + 2 * 16384 <= r_u + 4 * CW * 4
    xf = place("xf", [P, 3, D], at=r_q)
    yr = place("yr", [P, 3, D], at=r_q + 3 * D * 4)
    assert r_q + 6 * D * 4 <= r_p + 4096
    lnB = place("lnB", [P, 2, D], at=r_p + 4096)
    assert r_p + 4096 + 2 * D * 4 <= r_u
    gateB = place("gateB", [P, 2, D], at=r_u)
    w_raw = place("w_raw", [P, 2, KT, P])
    wo_raw = place("wo_raw", [P, 2, D], at=top[0] - 2 * D * 4)
    r_hl = region(4 * KT * P * 4)
    w_hi = place("w_hi", [P, 2, KT, P], F32R, at=r_hl)
    w_lo = place("w_lo", [P, 2, KT, P], F32R, at=r_hl + 2 * KT * P * 4)
    m_hi = place("m_hi", [P, 2, KT, P], F32R, at=r_hl)
    m_lo = place("m_lo", [P, 2, KT, P], F32R, at=r_hl + 2 * KT * P * 4)
    part = place("part", [P, 2, 512])
    wp = place("wp", [P, 4, P])
    vnew = place("vnew", [LS, NSEQ, P])
    ident = place("ident", [P, P])
    sel = place("sel", [P, 9])
    ebc = place("ebc", [P, 2, P])
    cT = place("cT", [P, KT, 9])
    thc = place("thc", [P, KT, 9])
    cpad = place("cpad", [P, KT, 32])
    bT = place("bT", [P, 24])
    shT = place("shT", [P, KT, 9])
    s1T = place("s1T", [P, KT, 9])
    psc = place("psc", [P, 4])
    psc2 = place("psc2", [P, 4])
    nsp = place("nsp", [P, 4])
    nss = place("nss", [P, 2])
    skp = place("skp", [P, 4])
    sks = place("sks", [P, 2])
    bnst = place("bnst", [P, 2, 12])
    mv = place("mv", [P, 2, 2])
    veps = place("veps", [P, 2 * TILES])
    nmu = place("nmu", [P, 2 * TILES])
    rstd = place("rstd", [P, 2 * TILES])
    nmr = place("nmr", [P, 2 * TILES])
    mhalf = place("mhalf", [P, 1])
    mxs = place("mxs", [P, 2, 4])
    negm = place("negm", [P, 2, 4])
    sdl = place("sdl", [P, 2, 4])
    es = place("es", [P, 2, 4])
    rs = place("rs", [P, 2, 4])
    den = place("den", [P, 2, 4])
    rden = place("rden", [P, 2, 4])
    invc = place("invc", [P, HIST])
    fix = place("fix", [P, HIST])

    proj_ps = nc.alloc_psum_tensor("proj_ps", [P, 3, 512], F32)
    s_ps = nc.alloc_psum_tensor("s_ps", [P, 2, 512], F32)
    t_ps = nc.alloc_psum_tensor("t_ps", [P, 2, 512], F32)
    o_ps = nc.alloc_psum_tensor("o_ps", [P, 512], F32)

    sem = nc.alloc_semaphore
    ld_c = sem("ld_c"); ld_id = sem("ld_id"); ld_small = sem("ld_small"); ld_cs = sem("ld_cs"); ld_brow = sem("ld_brow")
    ld_ada = [sem(f"ld_ada{i}") for i in range(3)]
    ld_x = [sem(f"ld_x{i}") for i in range(4)]
    ld_w = [sem(f"ld_w{i}") for i in range(2)]
    ld_kv = [sem(f"ld_kv{i}") for i in range(2)]
    ld_hist = sem("ld_hist"); ld_ln = sem("ld_ln")
    ld_xf = [sem(f"ld_xf{i}") for i in range(3)]
    st_y = [sem(f"st_y{i}") for i in range(3)]
    st_u = sem("st_u"); st_misc = sem("st_misc"); st_k = sem("st_k"); st_v = sem("st_v")
    ada_done = sem("ada_done"); sel_done = sem("sel_done"); xt_done = sem("xt_done"); unit_done = sem("unit_done")
    vt_done = sem("vt_done"); s_done = sem("s_done"); t_done = sem("t_done"); pv_done = sem("pv_done"); y_done = sem("y_done")
    thc_done = sem("thc_done"); xn_done = sem("xn_done"); ada_evac = sem("ada_evac"); xte_a = sem("xte_a")
    hhi_done = sem("hhi_done"); whi_done = sem("whi_done"); act_free = sem("act_free"); th_done = sem("th_done")
    exp_done = sem("exp_done"); es_done = sem("es_done"); pt1_done = sem("pt1_done"); mhi_done = sem("mhi_done"); yn_done = sem("yn_done")
    dve_step = sem("dve_step"); c_done = sem("c_done"); stats_done = sem("stats_done"); xte_v = sem("xte_v"); mod_done = sem("mod_done")
    hx_done = sem("hx_done"); hlo_v = sem("hlo_v"); dve_free = sem("dve_free"); rope_done = sem("rope_done"); mg_done = sem("mg_done")
    d_done = sem("d_done"); max_done = sem("max_done"); p_done = sem("p_done"); pt2_done = sem("pt2_done"); mix_done = sem("mix_done")
    vte_done = sem("vte_done"); mlo_done = sem("mlo_done"); r_done = sem("r_done"); g_done = sem("g_done"); wlo_v = sem("wlo_v"); consts_v = sem("consts_v")
    pool_step = sem("pool_step"); rstd_done = sem("rstd_done"); wlo_done = sem("wlo_done"); hlo_p = sem("hlo_p"); sum_done = sem("sum_done")
    yb_done = sem("yb_done")

    def cols(c):
        return slice(CW * c, CW * (c + 1))

    block = nc.Block()
    with block as block:

        @block.sync
        def _(sp):
            sp.dma_start(cT[:], cT_d).then_inc(ld_c, 16)
            sp.dma_start(wada[0][:], w_ada[ADA[0]]).then_inc(ld_ada[0], 16)

            def load_x(t):
                if t >= 4:
                    sp.wait_ge(xt_done, 2 * (t - 3))
                sp.dma_start(xs[:, t % 4, :], x_all[t]).then_inc(ld_x[t % 4], 16)

            def load_w(b):
                if b >= 2:
                    sp.wait_ge(whi_done, b - 1)
                    sp.wait_ge(wlo_done, b - 1)
                sp.dma_start(w_raw[:, b % 2], w_in[b]).then_inc(ld_w[b % 2], 16)

            def load_kv(p):
                if p >= 2:
                    sp.wait_ge(pv_done, NQ + p - 1)
                pair = slice(2 * p, 2 * p + 2)
                sp.dma_start(Ks[:, p % 2], kcT[pair].rearrange("s p t -> p s t")).then_inc(ld_kv[p % 2], 16)
                sp.dma_start(Vs[:, p % 2], vc[pair].rearrange("s p d -> p s d")).then_inc(ld_kv[p % 2], 16)

            def samples_u():
                return uext[:, UE:UW].rearrange("p (s t) -> p s t", t=HIST + LS)

            def load_history(g):
                if g == 0:
                    sp.wait_ge(rope_done, 15)
                else:
                    sp.wait_ge(d_done, g)
                    sp.wait_ge(st_u, 32 * g)
                sp.dma_start(samples_u()[:, :, 0:HIST], histT[g]).then_inc(ld_hist, 16)

            def store_u(g):
                sp.wait_ge(act_free, freed_count(unit_index("u", g, NCH - 1))[1])
                sp.dma_start(upT_out[g], uext[:, UE - HIST:UE]).then_inc(st_u, 16)
                sp.dma_start(usT_out[g], samples_u()[:, :, LS:HIST + LS]).then_inc(st_u, 16)

            load_x(0)
            sp.dma_start(ident[:], ident_d).then_inc(ld_id, 16)
            sp.dma_start(sel[:], sel_d).then_inc(ld_id, 16)
            sp.dma_start(bT[:], bT_d).then_inc(ld_id, 16)
            load_x(1)
            load_x(2)
            load_x(3)
            sp.dma_start(wada[1][:], w_ada[ADA[1]]).then_inc(ld_ada[1], 16)
            sp.wait_ge(ada_done, 1)
            sp.dma_start(wada[0][:], w_ada[ADA[2]]).then_inc(ld_ada[0], 16)
            sp.wait_ge(ada_done, 2)
            sp.dma_start(wada[1][:], w_ada[ADA[3]]).then_inc(ld_ada[1], 16)
            load_w(0)
            load_w(1)
            load_x(4)
            load_x(5)
            sp.wait_ge(ada_done, 3)
            sp.dma_start(cosT[:], cos_d).then_inc(ld_cs, 16)
            sp.dma_start(sinT[:], sin_d).then_inc(ld_cs, 16)
            load_x(6)
            load_x(7)
            load_x(8)
            load_w(2)
            sp.dma_start(ebc[:], ebc_d).then_inc(ld_small, 16)
            sp.dma_start(wp[:], w_pool).then_inc(ld_small, 16)
            sp.dma_start(psc[:], pscale_d).then_inc(ld_small, 16)
            sp.dma_start(skp[:], sinkp_d).then_inc(ld_small, 16)
            sp.dma_start(sks[:], sinks_d).then_inc(ld_small, 16)
            sp.dma_start(kcT_out, kc_tail).then_inc(st_misc, 16)
            sp.dma_start(vc_out, vc_tail).then_inc(st_misc, 16)
            load_w(3)
            sp.wait_ge(xt_done, 2 * TILES)
            sp.dma_start(wada_late[:], w_ada[ADA[4]]).then_inc(ld_ada[2], 16)
            load_w(4)
            sp.wait_ge(ada_done, 5)
            sp.dma_start(wada_late[:], w_ada[ADA[5]]).then_inc(ld_ada[2], 16)
            load_w(5)
            sp.wait_ge(ada_evac, 6)
            sp.dma_start(part[9:10, :, :], brow_d).then_inc(ld_brow, 16)
            for b in range(6, NBLK):
                load_w(b)
                if b == 7:
                    sp.wait_ge(rope_done, NCH)
                    sp.dma_start(kT_out, kT[:, SEQ - WIN:TOK]).then_inc(st_k, 16)
                    sp.wait_ge(act_free, NCH)
                    sp.dma_start(vT_out, vT[:, SEQ - WIN:TOK]).then_inc(st_v, 16)
                if b == 9:
                    load_kv(0)
                    load_kv(1)
                if b >= 11 and b % 2:
                    load_history((b - 11) // 2)
                if b >= 12 and b % 2 == 0:
                    store_u((b - 12) // 2)
            for k in range(KT):
                if k == 2:
                    store_u(3)
                b = NBLK + k
                sp.wait_ge(whi_done, b - 1)
                sp.wait_ge(wlo_done, b - 1) if k < 2 else sp.wait_ge(wlo_v if k % 2 == 0 else wlo_done, k // 2 if k % 2 == 0 else NBLK + k // 2)
                sp.dma_start(wo_raw[:, k % 2], w_out[k]).then_inc(ld_w[b % 2], 16)
            load_kv(2)
            load_kv(3)
            sp.wait_ge(st_k, 16)
            sp.wait_ge(pv_done, NSTEP)
            sp.wait_ge(s_done, NSTEP)
            sp.dma_start(lnB[:, 0, :], ln_g.to_broadcast([P, D])).then_inc(ld_ln, 16)
            sp.dma_start(lnB[:, 1, :], ln_b.to_broadcast([P, D])).then_inc(ld_ln, 16)
            for t in range(TILES):
                if t >= 3:
                    sp.wait_ge(r_done, t - 2)
                sp.dma_start(xf[:, t % 3, :], x_all[t]).then_inc(ld_xf[t % 3], 16)
                if t >= 2:
                    sp.wait_ge(yb_done, t - 1)
                    sp.dma_start(y_out[t - 2], yr[:, (t - 2) % 3, :]).then_inc(st_y[(t - 2) % 3], 16)
            for t in range(TILES - 2, TILES):
                sp.wait_ge(yb_done, t + 1)
                sp.dma_start(y_out[t], yr[:, t % 3, :]).then_inc(st_y[t % 3], 16)
            for i in range(3):
                sp.wait_ge(st_y[i], 16 * (TILES // 3))
            sp.wait_ge(st_u, 32 * 4)
            sp.wait_ge(st_misc, 16 * 2)

        @block.tensor
        def _(pe):
            def ada(a):
                s, n = (a % 2, a // 2 + 1) if a < 4 else (2, a - 3)
                w = wada[a % 2] if a < 4 else wada_late
                pe.wait_ge(ld_ada[s], 16 * n)
                if a == 0:
                    pe.wait_ge(c_done, 1)
                if a >= 2:
                    pe.wait_ge(ada_evac, a - 1)
                for k in range(KT):
                    g = 32 * (k % 4)
                    mm = pe.matmul(s_ps[g:g + 32, a % 2, :], cpad[:, k, :], w[:, k, :], start=(k < 4), stop=(k >= 4), tile_position=(0, g))
                mm.then_inc(ada_done, 1)

            def select(a):
                pe.wait_ge(ada_evac, a + 1)
                if a:
                    pe.wait_ge(mod_done, a)
                for m in range(4):
                    mm = pe.matmul(o_ps[:, 9 * m:9 * m + 9], part[:, a % 2, P * m:P * (m + 1)], sel[:], start=True, stop=True)
                mm.then_inc(sel_done, 1)

            def x_transpose(t):
                pe.wait_ge(xn_done, t + 1)
                if t == 0:
                    pe.wait_ge(ld_id, 48)
                for h in range(2):
                    if t:
                        pe.wait_ge(xte_a if h else xte_v, t)
                    for k in range(4):
                        mm = pe.transpose(t_ps[:, h, P * k:P * (k + 1)], xs[:, t % 4, P * (4 * h + k):P * (4 * h + k + 1)], ident[:])
                    mm.then_inc(xt_done, 1)

            def wait_bank(n):
                if n >= 3:
                    act, v = freed_count(n - 3)
                    pe.wait_ge(act_free if act else dve_free, v)

            def unit(n):
                kind, j, c = UNITS[n]
                bank = proj_ps[:, n % 3, :]
                wait_bank(n)
                if kind == "z":
                    pe.wait_ge(d_done, j + 1)
                    pe.wait_ge(ld_small, 80)
                    dd = sB if j % 2 == 0 else sA
                    mm = pe.matmul(bank[:, 0:CW], wp[:, j, :], dd[:, cols(c)], start=True, stop=True)
                elif kind == "r":
                    pe.wait_ge(ld_brow, 16)
                    mm = pe.matmul(bank[:], ebc[:, j, :], part[:, c, :], start=True, stop=True)
                else:
                    b = block_of(n)
                    if n == FIRST_UNIT[b]:
                        pe.wait_ge(whi_done, b + 1)
                        pe.wait_ge(wlo_done, b + 1)
                    for k in range(KT):
                        if kind == "k" and k % 2 == 0:
                            g = 4 * c + k // 2
                            pe.wait_ge(hhi_done, g + 1)
                            pe.wait_ge(hlo_p if g % 2 else hlo_v, g // 2 + 1)
                        hi, lo = h_hi[:, k, cols(c)], h_lo[:, k, cols(c)]
                        pe.matmul(bank[:, 0:CW], w_hi[:, b % 2, k, :], hi, start=(k == 0), stop=False)
                        pe.matmul(bank[:, 0:CW], w_hi[:, b % 2, k, :], lo, start=False, stop=False)
                        mm = pe.matmul(bank[:, 0:CW], w_lo[:, b % 2, k, :], hi, start=False, stop=(k == KT - 1))
                mm.then_inc(unit_done, 1)

            def v_transposes(m):
                pe.wait_ge(vte_done, m - 1) if m >= 2 else pe.wait_ge(xte_a if m else xte_v, TILES)
                if m == 0:
                    pe.wait_ge(act_free, NCH)
                for i in range(4):
                    if m < 4:
                        c = 4 * m + i
                        w = P if c < NQ - 1 else QB
                        mm = pe.transpose(t_ps[0:w, m % 2, P * i:P * (i + 1)], vT[:, QB * c:QB * c + w], ident[:])
                    else:
                        s = 4 * (m - 4) + i
                        mm = pe.transpose(t_ps[0:LS, m % 2, P * i:P * (i + 1)], vT[:, SEQ + LS * s:SEQ + LS * (s + 1)], ident[:])
                mm.then_inc(vt_done, 1)

            def scores(i):
                if i == 0:
                    pe.wait_ge(rope_done, 3 + 12)
                    pe.wait_ge(ada_evac, 6)
                else:
                    pe.wait_ge(exp_done, i)
                for kv in range(2):
                    r = slice(HD * kv, HD * (kv + 1))
                    if i < NQ:
                        nk = sum(keys_of(i))
                        k0 = QB * (i + 1) - nk
                        for p in range(2):
                            mm = pe.matmul(s_ps[:, kv, 192 * p:192 * p + nk], qP[r, i, 2 * p:2 * p + 2, :],
                                           kT[r, k0:k0 + nk], start=True, stop=True, tile_position=(HD * kv, 0))
                    else:
                        sp_ = i - NQ
                        if kv == 0:
                            pe.wait_ge(ld_kv[sp_ % 2], 32 * (sp_ // 2 + 1))
                        for e in range(2):
                            t0 = SEQ + LS * (2 * sp_ + e)
                            q = qS[r, 2 * sp_ + e, :, :]
                            o = s_ps[HD * e:HD * (e + 1), kv, :]
                            pe.matmul(o[:, 0:WIN], q, Ks[r, sp_ % 2, e, :], start=True, stop=True, tile_position=(HD * kv, HD * e))
                            mm = pe.matmul(o[:, WIN:WIN + LS], q, kT[r, t0:t0 + LS], start=True, stop=True, tile_position=(HD * kv, HD * e))
                mm.then_inc(s_done, 1)

            def p_transposes(i):
                pe.wait_ge(p_done, i + 1)
                if i:
                    pe.wait_ge(pt1_done, i)
                    if seconds(i - 1):
                        pe.wait_ge(pt2_done, seconds(i - 1))
                else:
                    pe.wait_ge(vte_done, 6)
                k1, k2 = keys_of(i)
                for j in range(4 if i < NQ else 2):
                    mm = pe.transpose(t_ps[0:k1, 0, P * j:P * (j + 1)], Pb[:, i % 2, j, 0:k1], ident[:])
                    if k2:
                        mm = pe.transpose(t_ps[0:k2, 1, P * j:P * (j + 1)], Pb[:, i % 2, j, WIN:WIN + k2], ident[:])
                mm.then_inc(t_done, 1)

            def values(i):
                pe.wait_ge(pt1_done, i + 1)
                if seconds(i):
                    pe.wait_ge(pt2_done, seconds(i))
                if i:
                    pe.wait_ge(mix_done, i)
                k1, k2 = keys_of(i)
                for kv in range(2):
                    d = slice(HD * kv, HD * (kv + 1))
                    if i < NQ:
                        o = o_ps[d, 0:256]
                        mm = pe.matmul(o, Vc[0:k1, max(i - 2, 0), d], PT1[0:k1, 256 * kv:256 * (kv + 1)], start=True, stop=not k2,
                                       tile_position=(0, HD * kv))
                        if k2:
                            mm = pe.matmul(o, Vc[0:QB, i, d], PT2[0:QB, 256 * kv:256 * (kv + 1)], start=False, stop=True,
                                           tile_position=(0, HD * kv))
                    else:
                        sp_ = i - NQ
                        for e in range(2):
                            o = o_ps[d, HD * e:HD * (e + 1)]
                            w = slice(P * kv + HD * e, P * kv + HD * (e + 1))
                            pe.matmul(o, Vs[:, sp_ % 2, e, d], PT1[:, w], start=True, stop=False, tile_position=(0, HD * kv))
                            mm = pe.matmul(o, vnew[0:LS, 2 * sp_ + e, d], PT2[0:LS, w], start=False, stop=True, tile_position=(0, HD * kv))
                mm.then_inc(pv_done, 1)

            def slot(i):
                if 0 <= i - 2 < NSTEP:
                    values(i - 2)
                if 0 <= i - 1 < NSTEP:
                    p_transposes(i - 1)
                if i < NSTEP:
                    scores(i)

            ada(0)
            x_transpose(0)
            x_transpose(1)
            x_transpose(2)
            x_transpose(3)
            ada(1)
            select(0)
            ada(2)
            select(1)
            ada(3)
            select(2)
            select(3)
            after = {0: [(x_transpose, 4), (x_transpose, 5)], 2: [(x_transpose, 6)], 3: [(x_transpose, 7), (x_transpose, 8)],
                     6: [(v_transposes, 0), (v_transposes, 1)], 7: [(ada, 4), (v_transposes, 2), (v_transposes, 3)],
                     8: [(v_transposes, 4), (v_transposes, 5)], 11: [(ada, 5)]}
            for n in range(NU):
                unit(n)
                for f, a in after.get(n, []):
                    f(a)
                for i in SLOTS.get(n, []):
                    slot(i)
            for t in range(TILES):
                pe.wait_ge(mhi_done, t + 1)
                pe.wait_ge(mlo_done, t + 1)
                if t >= 2:
                    pe.wait_ge(g_done, t - 1)
                elif t == 0:
                    pe.wait_ge(act_free, freed_count(NU - 1)[1])
                yb = proj_ps if t % 2 == 0 else s_ps
                for k in range(KT):
                    if t == 0:
                        pe.wait_ge(whi_done, NBLK + k + 1)
                        pe.wait_ge(wlo_v if k % 2 == 0 else wlo_done, (0 if k % 2 == 0 else NBLK) + k // 2 + 1)
                    for half in range(2):
                        o = yb[:, half, :]
                        w = slice(512 * half, 512 * (half + 1))
                        pe.matmul(o, m_hi[:, t % 2, k, :], wo_hi[:, k, w], start=(k == 0), stop=False)
                        pe.matmul(o, m_hi[:, t % 2, k, :], wo_lo[:, k, w], start=False, stop=False)
                        mm = pe.matmul(o, m_lo[:, t % 2, k, :], wo_hi[:, k, w], start=False, stop=(k == KT - 1))
                mm.then_inc(y_done, 1)

        @block.scalar
        def _(act):
            def normalise(t):
                act.wait_ge(rstd_done, t + 1)
                act.activation(xs[:, t % 4, :], xs[:, t % 4, :], ACT.Identity, bias=nmr[:, t:t + 1], scale=rstd[:, t:t + 1]).then_inc(xn_done, 1)

            def evac_ada(a):
                act.wait_ge(ada_done, a + 1)
                if a >= 2:
                    act.wait_ge(sel_done, min(a - 1, 4))
                act.activation(part[:, a % 2, :], s_ps[:, a % 2, :], ACT.Identity, scale=0.5).then_inc(ada_evac, 1)

            def evac_xt(t):
                act.wait_ge(xt_done, 2 * t + 2)
                act.activation(xnT[:, 4:8, P * t:P * (t + 1)], t_ps[:, 1, :].rearrange("p (k t) -> p k t", t=P), ACT.Copy).then_inc(xte_a, 1)

            def h_high(c):
                for g in range(4):
                    act.wait_ge(hx_done, 4 * c + g + 1)
                    act.activation(h_hi[:, 2 * g:2 * g + 2, cols(c)], xnT[:, 2 * g:2 * g + 2, cols(c)], ACT.Copy).then_inc(hhi_done, 1)

            def w_high(b):
                act.wait_ge(ld_w[b % 2], 16 * (b // 2 + 1))
                if b >= 2:
                    act.wait_ge(unit_done, LAST_UNIT[b - 2] + 1)
                act.activation(w_hi[:, b % 2], w_raw[:, b % 2], ACT.Copy).then_inc(whi_done, 1)

            def evac_unit(n):
                kind, j, c = UNITS[n]
                src = proj_ps[:, n % 3, 0:CW]
                if kind in ("k", "q", "z"):
                    return
                act.wait_ge(unit_done, n + 1)
                if kind == "v":
                    act.activation(vT[:, cols(c)], src, ACT.Copy).then_inc(act_free, 1)
                elif kind in ("ga", "gp"):
                    i = GATES.index(n)
                    if i >= 2:
                        act.wait_ge(dve_free, freed_count(GATES[i - 2])[1])
                    act.activation(th[:, i % 2, :], src, ACT.Tanh, scale=0.5).then_inc(th_done, 1)
                elif kind == "u":
                    if c == 0:
                        if j == 0:
                            act.wait_ge(rope_done, 15)
                        else:
                            act.wait_ge(d_done, j)
                            act.wait_ge(st_u, 32 * j)
                    if c < 2:
                        act.activation(uext[:, HIST + CW * c:HIST + CW * (c + 1)], src, ACT.Copy).then_inc(act_free, 1)
                    else:
                        act.activation(uext[:, HIST + 2 * CW:UE], src[:, 0:PW2], ACT.Copy)
                        act.activation(uext[:, UE:UW].rearrange("p (s t) -> p s t", t=HIST + LS)[:, :, HIST:],
                                       src[:, PW2:CW].rearrange("p (s t) -> p s t", t=LS), ACT.Copy).then_inc(act_free, 1)
                else:
                    if j == 0 and c == 0:
                        act.wait_ge(unit_done, unit_index("z", 3, 2) + 1)
                        act.wait_ge(st_u, 32 * 4)
                    act.activation(gateB[:, j, 512 * c:512 * (c + 1)], proj_ps[:, n % 3, :], ACT.Copy).then_inc(act_free, 1)

            def slot(i):
                if 0 <= i - 1 < NSTEP:
                    k1, _ = keys_of(i - 1)
                    w = 512 if i - 1 < NQ else 256
                    act.wait_ge(t_done, i)
                    if i >= 2:
                        act.wait_ge(pv_done, i - 1)
                    act.activation(PT1[0:k1, 0:w], t_ps[0:k1, 0, 0:w], ACT.Copy).then_inc(pt1_done, 1)
                if i < NSTEP:
                    act.wait_ge(max_done, i + 1)
                    if i == 0:
                        act.wait_ge(st_v, 16)
                    if i >= 2:
                        act.wait_ge(t_done, i - 1)
                        act.wait_ge(p_done, i - 1)
                    nj, nk = (4 if i < NQ else 2), sum(keys_of(i))
                    act.activation(es[:, i % 2, 0:nj], sdl[:, i % 2, 0:nj], ACT.Exp).then_inc(es_done, 1)
                    for j in range(nj):
                        src = s_ps[:, j // 2, 192 * (j % 2):192 * (j % 2) + nk] if i < NQ else s_ps[:, j, 0:nk]
                        e = act.activation(Pb[:, i % 2, j, 0:nk], src, ACT.Exp, bias=negm[:, i % 2, j:j + 1], scale=SCALE,
                                           accum_out=rs[:, i % 2, j:j + 1])
                    e.then_inc(exp_done, 1)

            act.wait_ge(ld_c, 16)
            act.activation(thc[:], cT[:], ACT.Tanh, scale=0.5).then_inc(thc_done, 1)
            normalise(0)
            evac_ada(0)
            normalise(1)
            evac_xt(0)
            normalise(2)
            evac_xt(1)
            normalise(3)
            evac_xt(2)
            evac_xt(3)
            evac_ada(1)
            evac_ada(2)
            evac_ada(3)
            w_high(0)
            w_high(1)
            h_high(0)
            normalise(4)
            normalise(5)
            evac_xt(4)
            evac_xt(5)
            h_high(1)
            evac_unit(1)
            normalise(6)
            evac_xt(6)
            normalise(7)
            normalise(8)
            evac_unit(3)
            evac_xt(7)
            evac_xt(8)
            h_high(2)
            w_high(2)
            evac_unit(5)
            w_high(3)
            after = {7: 4, 11: 5}
            for n in range(6, NU):
                b = block_of(n)
                evac_unit(n)
                if n in after:
                    evac_ada(after[n])
                for i in SLOTS.get(n, []):
                    slot(i)
                if b is not None and LAST_UNIT[b] == n and b + 2 < NBLK:
                    w_high(b + 2)
                if n == LAST_PROJ:
                    for k in range(KT):
                        i = NBLK + k
                        act.wait_ge(ld_w[i % 2], 16 * (i // 2 + 1))
                        act.activation(wo_hi[:, k, :], wo_raw[:, k % 2, :], ACT.Copy).then_inc(whi_done, 1)

            def mixed_high(t):
                if t == 0:
                    act.wait_ge(mix_done, NSTEP)
                    act.wait_ge(dve_free, freed_count(unit_index("z", 3, 2))[1])
                if t >= 2:
                    act.wait_ge(y_done, t - 1)
                act.activation(m_hi[:, t % 2], mixed[:, :, P * t:P * (t + 1)], ACT.Copy).then_inc(mhi_done, 1)

            mixed_high(0)
            mixed_high(1)
            for t in range(TILES):
                act.wait_ge(rstd_done, TILES + t + 1)
                act.activation(yr[:, t % 3, :], yr[:, t % 3, :], ACT.Identity, bias=nmr[:, TILES + t:TILES + t + 1],
                               scale=rstd[:, TILES + t:TILES + t + 1]).then_inc(yn_done, 1)
                if t + 2 < TILES:
                    mixed_high(t + 2)

        @block.vector
        def _(dve):
            steps = [0]

            def link(ins):
                steps[0] += 1
                ins.then_inc(dve_step, 1)
                dve.wait_ge(dve_step, steps[0])

            def stats(t, src):
                b = t % 2
                dve.bn_stats(bnst[:, b, 0:6], src[:, 0:512])
                link(dve.bn_stats(bnst[:, b, 6:12], src[:, 512:1024]))
                link(dve.bn_aggr(mv[:, b, :], bnst[:, b, :]))
                dve.tensor_scalar(nmu[:, t:t + 1], mv[:, b, 0:1], -1.0, None, ALU.mult)
                dve.tensor_scalar(veps[:, t:t + 1], mv[:, b, 1:2], EPS, None, ALU.add).then_inc(stats_done, 1)

            def x_stats(t):
                dve.wait_ge(ld_x[t % 4], 16 * (t // 4 + 1))
                stats(t, xs[:, t % 4, :])

            def evac_xt(t):
                dve.wait_ge(xt_done, 2 * t + 1)
                dve.tensor_copy(xnT[:, 0:4, P * t:P * (t + 1)], t_ps[:, 0, :].rearrange("p (k t) -> p k t", t=P)).then_inc(xte_v, 1)

            def modulation(a):
                dve.wait_ge(sel_done, a + 1)
                if a == 0:
                    dve.wait_ge(ld_id, 48)
                ci = ADA[a]
                dst = shT if ci < 2 else s1T
                k0 = 4 * (ci % 2)
                dve.scalar_tensor_tensor(dst[:, k0:k0 + 4, :], o_ps[:, 0:36].rearrange("p (k s) -> p k s", s=9), 0.0 if ci < 2 else 1.0,
                                         bT[:, 4 * ci:4 * ci + 4].unsqueeze(2).to_broadcast([P, 4, 9]), ALU.add, ALU.add).then_inc(mod_done, 1)

            def h_chunk(c):
                if c == 0:
                    dve.wait_ge(mod_done, 4)
                dve.wait_ge(xte_a, 3 * c + 3)
                dve.wait_ge(xte_v, 3 * c + 3)
                pw = CW if c < 2 else PW2
                if c == 2:
                    v = xnT[:, :, SEQ:TOK].rearrange("p k (s t) -> p k s t", t=LS)
                    for src, op in ((s1T, ALU.mult), (shT, ALU.add)):
                        for k in range(KT):
                            last = dve.tensor_tensor(v[:, k], v[:, k], src[:, k, 1:9].unsqueeze(2).to_broadcast([P, NSEQ, LS]), op)
                        link(last)
                for g in range(4):
                    for k in (2 * g, 2 * g + 1):
                        x = xnT[:, k, CW * c:CW * c + pw]
                        last = dve.tensor_scalar(x, x, s1T[:, k, 0:1], shT[:, k, 0:1], ALU.mult, ALU.add)
                    last.then_inc(hx_done, 1)
                    if g % 2 == 0:
                        dve.wait_ge(hhi_done, 4 * c + g + 1)
                        w = slice(2 * g, 2 * g + 2)
                        dve.tensor_tensor(h_lo[:, w, cols(c)], xnT[:, w, cols(c)], h_hi[:, w, cols(c)].bitcast(F32), ALU.subtract).then_inc(hlo_v, 1)

            def evac_unit(n):
                kind, j, c = UNITS[n]
                src = proj_ps[:, n % 3, 0:CW]
                if kind in ("v", "u", "r"):
                    return
                if kind in ("k", "q"):
                    i = count(("k", "q"), n) - 1
                    if i == 0:
                        dve.wait_ge(ld_cs, 32)
                    if kind == "q" and j == 0 and c == 0:
                        dve.wait_ge(ada_done, 6)
                    dve.wait_ge(unit_done, n + 1)
                    r = i % 2
                    dve.stream_shuffle(rt1[:, r, :], src, [(m + 16) % 32 for m in range(32)])
                    dve.tensor_tensor(rt2[:, r, :], src, cosT[:, cols(c)], ALU.mult).then_inc(dve_free, 1)
                    dve.wait_ge(dve_free, freed_count(n)[1])
                    link(dve.tensor_tensor(rt1[:, r, :], rt1[:, r, :], sinT[:, cols(c)], ALU.mult))
                    if kind == "k":
                        dve.tensor_tensor(kT[:, cols(c)], rt1[:, r, :], rt2[:, r, :], ALU.add).then_inc(rope_done, 1)
                        return
                    pw = CW if c < 2 else PW2
                    nq = CW // QB
                    a, b = (x[:, r, 0:pw].rearrange("p (q t) -> p q t", t=QB) for x in (rt1, rt2))
                    last = dve.tensor_tensor(qP[:, nq * c:nq * c + pw // QB, j, :], a, b, ALU.add)
                    if c == 2:
                        a, b = (x[:, r, pw:CW].rearrange("p (s t) -> p s t", t=LS) for x in (rt1, rt2))
                        last = dve.tensor_tensor(qS[:, :, j, :], a, b, ALU.add)
                    last.then_inc(rope_done, 1)
                elif kind in ("ga", "gp"):
                    i = count(("ga", "gp"), n) - 1
                    dve.wait_ge(th_done, i + 1)
                    if n == FIRST_UNIT[GA_BLK[0]]:
                        dve.wait_ge(hlo_p, 6)
                        dve.wait_ge(hhi_done, 12)
                    dst = mixed[:, j if kind == "ga" else 4 + j, cols(c)]
                    dve.scalar_tensor_tensor(dst, th[:, i % 2, :], 1.0, src, ALU.add, ALU.mult).then_inc(dve_free, 1)
                else:
                    dve.wait_ge(unit_done, n + 1)
                    dve.wait_ge(dve_free, freed_count(unit_index("gp", j, c))[1])
                    dst = mixed[:, 4 + j, cols(c)]
                    dve.scalar_tensor_tensor(dst, src, psc2[:, j:j + 1], dst, ALU.mult, ALU.mult).then_inc(dve_free, 1)

            def pool_mean(g):
                w = 2 << g
                s, d = (sA, sB) if g % 2 == 0 else (sB, sA)
                dve.wait_ge(sum_done, g + 1)
                link(dve.tensor_tensor(fix[:, 0:w - 1], s[:, HIST:HIST + w - 1], invc[:, 0:w - 1], ALU.mult))
                dve.scalar_tensor_tensor(d[:, w - 1:SEQ], s[:, HIST + w - 1:UE], 1.0 / w, uext[:, HIST + w - 1:UE], ALU.mult, ALU.subtract)
                dve.tensor_tensor(d[:, 0:w - 1], fix[:, 0:w - 1], uext[:, HIST:HIST + w - 1], ALU.subtract)

                def samples(x):
                    return x[:, UE:UW].rearrange("p (s t) -> p s t", t=HIST + LS)[:, :, HIST:]

                dve.scalar_tensor_tensor(d[:, SEQ:TOK].rearrange("p (s t) -> p s t", t=LS), samples(s), 1.0 / w, samples(uext),
                                         ALU.mult, ALU.subtract).then_inc(d_done, 1)

            def evac_v(m):
                dve.wait_ge(vt_done, m + 1)
                if m < 4:
                    if m < 3:
                        dve.tensor_copy(Vc[:, 4 * m:4 * m + 4, :], t_ps[:, m % 2, :].rearrange("p (c d) -> p c d", d=P)).then_inc(vte_done, 1)
                    else:
                        dve.tensor_copy(Vc[:, 12:15, :], t_ps[:, 1, 0:3 * P].rearrange("p (c d) -> p c d", d=P))
                        dve.tensor_copy(Vc[0:QB, 15, :], t_ps[0:QB, 1, 3 * P:4 * P]).then_inc(vte_done, 1)
                else:
                    dve.tensor_copy(vnew[:, 4 * (m - 4):4 * (m - 3), :], t_ps[0:LS, m % 2, :].rearrange("p (c d) -> p c d", d=P)).then_inc(vte_done, 1)

            def mix(i):
                dve.wait_ge(pv_done, i + 1)
                if i < NQ:
                    g = mixed[:, 0:4, QB * i:QB * (i + 1)]
                    dve.scalar_tensor_tensor(g, o_ps[:, 0:256].rearrange("p (j t) -> p j t", t=QB), 0.5, g, ALU.mult, ALU.mult).then_inc(mix_done, 1)
                else:
                    for e in range(2):
                        t0 = SEQ + LS * (2 * (i - NQ) + e)
                        g = mixed[:, 0:4, t0:t0 + LS]
                        last = dve.scalar_tensor_tensor(g, o_ps[:, HD * e:HD * (e + 1)].rearrange("p (j t) -> p j t", t=LS), 0.5, g, ALU.mult, ALU.mult)
                    last.then_inc(mix_done, 1)

            def slot(i):
                if 0 <= i - 2 < NSTEP:
                    mix(i - 2)
                if 0 <= i - 1 < NSTEP and keys_of(i - 1)[1]:
                    k2 = keys_of(i - 1)[1]
                    w = 512 if i - 1 < NQ else 256
                    dve.wait_ge(t_done, i)
                    if i >= 2:
                        dve.wait_ge(pv_done, i - 1)
                    dve.tensor_copy(PT2[0:k2, 0:w], t_ps[0:k2, 1, 0:w]).then_inc(pt2_done, 1)
                if i < NSTEP:
                    b, nk = i % 2, sum(keys_of(i))
                    dve.wait_ge(s_done, i + 1)
                    if i < NQ:
                        nj, sink = 4, nsp
                        src = s_ps[:, :, 0:384].rearrange("p b (r n) -> p b r n", n=192)[:, :, :, 0:nk]
                        out = mxs[:, b, :].rearrange("p (b r) -> p b r", r=2)
                    else:
                        nj, sink = 2, nss
                        src, out = s_ps[:, :, 0:nk], mxs[:, b, 0:2]
                    link(dve.tensor_reduce(out, src, AX.X, ALU.max))
                    link(dve.scalar_tensor_tensor(negm[:, b, 0:nj], mxs[:, b, 0:nj], -SCALE, sink[:, 0:nj], ALU.mult, ALU.min))
                    dve.tensor_tensor(sdl[:, b, 0:nj], negm[:, b, 0:nj], sink[:, 0:nj], ALU.subtract).then_inc(max_done, 1)
                    dve.wait_ge(exp_done, i + 1)
                    dve.wait_ge(es_done, i + 1)
                    link(dve.tensor_tensor(den[:, b, 0:nj], rs[:, b, 0:nj], es[:, b, 0:nj], ALU.add))
                    link(dve.reciprocal(rden[:, b, 0:nj], den[:, b, 0:nj]))
                    p = Pb[:, b, 0:nj, 0:nk]
                    dve.tensor_tensor(p, p, rden[:, b, 0:nj].unsqueeze(2).to_broadcast([P, nj, nk]), ALU.mult).then_inc(p_done, 1)

            link(dve.memset(cpad[:], 0.0))
            dve.memset(mhalf[:], -0.5).then_inc(consts_v, 1)
            dve.wait_ge(thc_done, 1)
            dve.scalar_tensor_tensor(cpad[:, :, 0:9], thc[:], 1.0, cT[:], ALU.add, ALU.mult).then_inc(c_done, 1)
            for m in range(HIST):
                last = dve.memset(invc[:, m:m + 1], 1.0 / (m + 1))
            link(last)
            x_stats(0)
            x_stats(1)
            evac_xt(0)
            x_stats(2)
            evac_xt(1)
            x_stats(3)
            evac_xt(2)
            evac_xt(3)
            for a in range(4):
                modulation(a)
            h_chunk(0)
            x_stats(4)
            x_stats(5)
            evac_unit(0)
            evac_xt(4)
            evac_xt(5)
            h_chunk(1)
            x_stats(6)
            x_stats(7)
            x_stats(8)
            evac_unit(2)
            evac_xt(6)
            evac_xt(7)
            evac_xt(8)
            h_chunk(2)
            evac_unit(4)
            after = {6: [0, 1], 7: [2, 3], 8: [4, 5]}
            for n in range(6, NU):
                if n == 9:
                    dve.wait_ge(ld_small, 16 * 5)
                    dve.tensor_scalar(psc2[:], psc[:], 0.5, None, ALU.mult)
                    dve.tensor_scalar(nsp[:], skp[:], -1.0, None, ALU.mult)
                    link(dve.tensor_scalar(nss[:], sks[:], -1.0, None, ALU.mult))
                kind, j, c = UNITS[n]
                if kind == "z" and c == 0:
                    pool_mean(j)
                evac_unit(n)
                for m in after.get(n, []):
                    evac_v(m)
                for i in SLOTS.get(n, []):
                    slot(i)
                if n == LAST_PROJ:
                    for k in range(0, KT, 2):
                        dve.wait_ge(whi_done, NBLK + k + 1)
                        dve.tensor_tensor(wo_lo[:, k, :], wo_raw[:, k % 2, :], wo_hi[:, k, :].bitcast(F32), ALU.subtract).then_inc(wlo_v, 1)

            def mixed_low(t):
                dve.wait_ge(mhi_done, t + 1)
                dve.tensor_tensor(m_lo[:, t % 2], mixed[:, :, P * t:P * (t + 1)], m_hi[:, t % 2].bitcast(F32), ALU.subtract).then_inc(mlo_done, 1)

            mixed_low(0)
            mixed_low(1)
            for t in range(TILES):
                yb = proj_ps if t % 2 == 0 else s_ps
                r = yr[:, t % 3, :]
                row = 0 if t < TILES - 1 else 1
                dve.wait_ge(y_done, t + 1)
                if t >= 3:
                    dve.wait_ge(st_y[t % 3], 16 * (t // 3))
                dve.tensor_tensor(r.rearrange("p (h n) -> p h n", n=512), yb[:, 0:2, :], gateB[:, row, :].rearrange("p (h n) -> p h n", n=512),
                                  ALU.mult).then_inc(g_done, 1)
                dve.wait_ge(g_done, t + 1)
                dve.wait_ge(ld_xf[t % 3], 16 * (t // 3 + 1))
                dve.scalar_tensor_tensor(r, xf[:, t % 3, :], ALPHA, r, ALU.mult, ALU.add).then_inc(r_done, 1)
                dve.wait_ge(r_done, t + 1)
                stats(TILES + t, r)
                if t + 2 < TILES:
                    mixed_low(t + 2)
                dve.wait_ge(yn_done, t + 1)
                if t == 0:
                    dve.wait_ge(ld_ln, 32)
                dve.tensor_tensor(r, r, lnB[:, 0, :], ALU.mult).then_inc(mg_done, 1)

        @block.gpsimd
        def _(pool):
            steps = [0]

            def link(ins):
                steps[0] += 1
                ins.then_inc(pool_step, 1)
                pool.wait_ge(pool_step, steps[0])

            def inv_std(t):
                pool.wait_ge(stats_done, t + 1)
                link(pool.tensor_tensor(rstd[:, t:t + 1], veps[:, t:t + 1], mhalf[:], ALU.pow))
                pool.tensor_tensor(nmr[:, t:t + 1], nmu[:, t:t + 1], rstd[:, t:t + 1], ALU.mult).then_inc(rstd_done, 1)

            def w_low(b):
                pool.wait_ge(whi_done, b + 1)
                pool.tensor_tensor(w_lo[:, b % 2], w_raw[:, b % 2], w_hi[:, b % 2].bitcast(F32), ALU.subtract).then_inc(wlo_done, 1)

            def h_low(c):
                for g in (1, 3):
                    pool.wait_ge(hhi_done, 4 * c + g + 1)
                    w = slice(2 * g, 2 * g + 2)
                    pool.tensor_tensor(h_lo[:, w, cols(c)], xnT[:, w, cols(c)], h_hi[:, w, cols(c)].bitcast(F32), ALU.subtract).then_inc(hlo_p, 1)

            def window_sums(g):
                if g == 0:
                    pool.wait_ge(rope_done, 15)
                    link(pool.memset(uext[:, 0:HIST], 0.0))
                pool.wait_ge(act_free, freed_count(unit_index("u", g, NCH - 1))[1])
                pool.wait_ge(ld_hist, 16 * (g + 1))
                if g:
                    pool.wait_ge(unit_done, unit_index("z", g - 1, NCH - 1) + 1)
                src, lag = uext, 1
                for m in range(g + 1):
                    dst = sA if m % 2 == 0 else sB
                    first = 2 * lag - 1
                    ins = pool.tensor_tensor(dst[:, first:UW], src[:, first:UW], src[:, first - lag:UW - lag], ALU.add)
                    if m < g:
                        link(ins)
                    src, lag = dst, 2 * lag
                ins.then_inc(sum_done, 1)

            pool.wait_ge(consts_v, 1)
            for t in range(4):
                inv_std(t)
            w_low(0)
            w_low(1)
            h_low(0)
            inv_std(4)
            inv_std(5)
            h_low(1)
            inv_std(6)
            inv_std(7)
            inv_std(8)
            h_low(2)
            w_low(2)
            w_low(3)
            for b in range(4, NBLK):
                w_low(b)
                if b in (12, 14, 16, 17):
                    window_sums((b - 11) // 2)
            for k in range(1, KT, 2):
                pool.wait_ge(whi_done, NBLK + k + 1)
                pool.tensor_tensor(wo_lo[:, k, :], wo_raw[:, k % 2, :], wo_hi[:, k, :].bitcast(F32), ALU.subtract).then_inc(wlo_done, 1)
            for t in range(TILES):
                inv_std(TILES + t)
                pool.wait_ge(mg_done, t + 1)
                pool.tensor_tensor(yr[:, t % 3, :], yr[:, t % 3, :], lnB[:, 1, :], ALU.add).then_inc(yb_done, 1)



def head_dims():
    return np.concatenate([np.r_[16 * q:16 * q + 16, 32 + 16 * q:32 + 16 * q + 16] for q in range(2)])


def projection_columns():
    perm = head_dims()
    pair = [np.r_[HD * j:HD * (j + 1), HD * (4 + j):HD * (5 + j)] for j in range(4)]
    qpair = [np.r_[HD * j + perm, HD * (4 + j) + perm] for j in range(4)]
    k = 512 + np.r_[perm, HD + perm]
    v = 640 + np.arange(P)
    ga = [768 + p for p in pair]
    pooled = [a for g in range(4) for a in (1280 + P * g + np.arange(P), 1792 + P * g + np.arange(P))]
    return np.concatenate([k, v, *ga, *qpair, *pooled])


def tables():
    pos = np.concatenate([np.arange(SEQ), np.tile(1024 + np.arange(LS), NSEQ)]).astype(np.float32)
    half = HD // 2
    inv = (np.float32(10000.0) ** (-np.arange(half, dtype=np.float32) / np.float32(half))).astype(np.float32)
    ang = inv[:, None] * pos[None, :]
    perm = head_dims()
    rows = np.r_[perm, perm]
    cos = np.cos(ang).astype(np.float32)[rows % half]
    sin = np.sin(ang).astype(np.float32)[rows % half] * np.where(rows < half, -1.0, 1.0).astype(np.float32)[:, None]
    ident = np.eye(P, dtype=np.float32)
    sel = np.zeros((P, 9), np.float32)
    ebc = np.zeros((P, 2, P), np.float32)
    for g in range(4):
        for s in range(9):
            sel[32 * g + s, s] = 1.0
        ebc[32 * g, 0, :] = 1.0
        for s in range(NSEQ):
            ebc[32 * g + 1 + s, 1, LS * s:LS * (s + 1)] = 1.0
    ebc[9, :, :] = 1.0
    return cos, np.ascontiguousarray(sin), ident, sel, ebc


def kernel(x_prompt, x_sample, cache_k, cache_v, state_pool, c_prompt, c_sample, w_ada, b_ada, w_in, attn_sinks, w_pool,
           pool_scale, w_out, ln_g, ln_b):
    import concourse.bacc as bacc
    from concourse.bass_utils import run_bass_kernel_spmd

    A = np.asarray
    cos, sin, ident, sel, ebc = tables()
    perm = head_dims()
    c_all = np.concatenate([A(c_prompt), A(c_sample)], 0)
    sinks = A(attn_sinks)[0]
    kc = A(cache_k)[0][..., perm].reshape(NSEQ, WIN, P)
    vcn = A(cache_v)[0].reshape(NSEQ, WIN, P)
    pair = np.concatenate([np.r_[HD * j:HD * (j + 1), HD * (4 + j):HD * (5 + j)] for j in range(4)])
    arrays = {
        "x_all": np.concatenate([A(x_prompt)[0], A(x_sample).reshape(-1, D)], 0).reshape(TILES, P, D),
        "cT_d": c_all.T.reshape(KT, P, 9).transpose(1, 0, 2),
        "bT_d": A(b_ada)[0].reshape(24, P).T,
        "w_ada": A(w_ada)[0].reshape(KT, P, 6, 512).transpose(2, 1, 0, 3),
        "w_in": A(w_in)[0][:, projection_columns()].reshape(KT, P, NBLK, P).transpose(2, 1, 0, 3),
        "w_out": A(w_out)[0][np.r_[pair, 512:1024]].reshape(KT, P, D),
        "w_pool": A(w_pool)[0].transpose(1, 0, 2),
        "pscale_d": A(pool_scale)[0].reshape(4, P).T,
        "sinkp_d": np.repeat(sinks.reshape(4, 2).T, QB, axis=0),
        "sinks_d": np.tile(np.repeat(sinks.reshape(2, 4).T, LS, axis=0), (2, 1)),
        "kcT": kc.transpose(0, 2, 1),
        "vc": vcn,
        "kc_tail": kc[:, LS:, :],
        "vc_tail": vcn[:, LS:, :],
        "histT": A(state_pool)[0].reshape(NSEQ, HIST, 4, P).transpose(2, 3, 0, 1),
        "ln_g": A(ln_g).reshape(1, D),
        "ln_b": A(ln_b).reshape(1, D),
        "ident_d": ident, "sel_d": sel, "ebc_d": ebc,
        "brow_d": A(b_ada)[0][2 * D:].reshape(1, 2, 512),
        "cos_d": cos, "sin_d": sin,
    }
    outs = {
        "y_out": (TILES, P, D), "kT_out": (P, 2 * WIN), "vT_out": (P, 2 * WIN), "upT_out": (4, P, HIST),
        "usT_out": (4, P, NSEQ, HIST), "kcT_out": (NSEQ, WIN - LS, P), "vc_out": (NSEQ, WIN - LS, P),
    }
    nc = bacc.Bacc("TRN2", target_bir_lowering=False, num_devices=1, dynamic_dma_scratch_size=1024)
    arrays = {n: np.ascontiguousarray(a) for n, a in arrays.items()}
    args = {n: nc.dram_tensor(n, a.shape, mybir.dt.from_np(a.dtype), kind="ExternalInput").ap() for n, a in arrays.items()}
    args.update({n: nc.dram_tensor(n, s, F32, kind="ExternalOutput").ap() for n, s in outs.items()})
    hybrid_step(nc, **args)
    r = run_bass_kernel_spmd(nc, [arrays], core_ids=[0]).results[0]

    inv = np.argsort(perm)
    y = r["y_out"].reshape(TOK, D)
    kn = r["kT_out"].T.reshape(2 * WIN, 2, HD)[..., inv]
    vn = r["vT_out"].T.reshape(2 * WIN, 2, HD)

    def sample_cache(old, new):
        return np.concatenate([old.reshape(NSEQ, WIN - LS, 2, HD), new[WIN:].reshape(NSEQ, LS, 2, HD)], 1)[None]

    up = r["upT_out"].transpose(2, 0, 1).reshape(1, 1, HIST, 512)
    us = r["usT_out"].transpose(2, 3, 0, 1).reshape(1, NSEQ, HIST, 512)
    return (y[:SEQ].reshape(1, SEQ, D), y[SEQ:].reshape(NSEQ, LS, D), kn[None, None, :WIN], vn[None, None, :WIN], up,
            sample_cache(r["kcT_out"].reshape(NSEQ, WIN - LS, 2, HD)[..., inv], kn), sample_cache(r["vc_out"], vn), us)
```

```python
import concourse.bass as bass
from concourse import mybir
import numpy as np

F32 = mybir.dt.float32
F32R = mybir.dt.float32r
ALU = mybir.AluOpType
ACT = mybir.ActivationFunctionType
AX = mybir.AxisListType

P = 128
D = 1024
SEQ = 1024
NSEQ = 8
LS = 16
TOK = SEQ + NSEQ * LS
KT = D // P
TILES = TOK // P
NCH = 3
CW = TOK // NCH
PW2 = SEQ - 2 * CW
HD = 64
QB = 64
NQ = 16
WIN = 128
HIST = 15
NSP = NSEQ // 2
NSTEP = NQ + NSP
ALPHA = float(2.0 ** 0.25)
EPS = 1e-5
SCALE = HD ** -0.5
UE = HIST + SEQ
UW = UE + NSEQ * (HIST + LS)
UB = (UW + 7) // 8 * 8

ADA = [0, 2, 1, 3, 4, 5]

K_BLK, V_BLK = 0, 1
GA_BLK = [2, 3, 4, 5]
Q_BLK = [6, 7, 8, 9]
GROUPS = [3, 2, 1, 0]
U_BLK = [10 + 2 * GROUPS.index(g) for g in range(4)]
GP_BLK = [11 + 2 * GROUPS.index(g) for g in range(4)]
NBLK = 18
RAW = 4
XS = 6
KVS = 4


def unit_list():
    units = []
    for c in range(NCH):
        units += [("k", 0, c), ("v", 0, c)]
    units += [("ga", j, c) for j in range(4) for c in range(NCH)]
    units += [("q", j, c) for j in range(4) for c in range(NCH)]
    for s, g in enumerate(GROUPS):
        for c in range(NCH):
            units.append(("u", g, c))
            if s and c == 0:
                units += [("z", GROUPS[s - 1], i) for i in range(NCH)]
        units += [("gp", g, c) for c in range(NCH - 1)]
        if s == 3:
            units += [("r", row, half) for row in range(2) for half in range(2)]
        units.append(("gp", g, NCH - 1))
    units += [("z", GROUPS[3], c) for c in range(NCH)]
    return units


UNITS = unit_list()
NU = len(UNITS)
BLOCK_OF = {"k": [K_BLK], "v": [V_BLK], "ga": GA_BLK, "q": Q_BLK, "u": U_BLK, "gp": GP_BLK}


def block_of(n):
    kind, j, _ = UNITS[n]
    return BLOCK_OF[kind][j] if kind in BLOCK_OF else None


LAST_UNIT = {block_of(n): n for n in range(NU) if block_of(n) is not None}
FIRST_UNIT = {block_of(n): n for n in reversed(range(NU)) if block_of(n) is not None}
LAST_PROJ = max(LAST_UNIT.values())
FREED_BY_ACT = ("v", "u", "r")


def freed_count(n):
    act = UNITS[n][0] in FREED_BY_ACT
    return act, sum((UNITS[m][0] in FREED_BY_ACT) == act for m in range(n + 1))


def count(kinds, n):
    return sum(UNITS[m][0] in kinds for m in range(n + 1))


def unit_index(kind, j, c):
    return UNITS.index((kind, j, c))


GATES = [n for n in range(NU) if UNITS[n][0] in ("ga", "gp")]

PLACES = [n for n in range(28, LAST_PROJ) if block_of(n) is not None] + [NU + m for m in range(2 * TILES)]
SLOTS = {PLACES[(5 * s) // 4]: [s] for s in range(NSTEP + 2)}


def keys_of(i):
    if i >= NQ:
        return WIN, LS
    nk = min(i + 1, 3) * QB
    return min(nk, WIN), max(nk - WIN, 0)


def seconds(i):
    return sum(keys_of(s)[1] > 0 for s in range(i + 1))


def hybrid_step(nc, x_all, cT_d, bT_d, w_ada, w_in, w_out, w_pool, pscale_d, sinkp_d, sinks_d, kcT, vc, kc_tail, vc_tail,
                histT, ln_g, ln_b, ident_d, sel_d, ebc_d, brow_d, cos_d, sin_d,
                y_out, kT_out, vT_out, upT_out, usT_out, kcT_out, vc_out):
    top = [nc.sbuf_base + 31 & ~31]

    def place(name, shape, dt=F32, at=None):
        size = 4
        for s in shape[1:]:
            size *= s
        if at is None:
            at = top[0]
            top[0] = (at + size + 31) & ~31
        return nc.alloc_sbuf_tensor_at(name, shape, dt, offset=at)

    def region(size):
        at = top[0]
        top[0] = (at + size + 31) & ~31
        return at

    r_h = region(2 * KT * TOK * 4)
    h_hi = place("h_hi", [P, KT, TOK], F32R, at=r_h)
    h_lo = place("h_lo", [P, KT, TOK], F32R, at=r_h + KT * TOK * 4)
    wo_hi = place("wo_hi", [P, KT, D], F32R, at=r_h)
    wo_lo = place("wo_lo", [P, KT, D], F32R, at=r_h + KT * TOK * 4)
    r_mx = region(KT * TOK * 4)
    xnT = place("xnT", [P, KT, TOK], at=r_mx)
    mixed = place("mixed", [P, KT, TOK], at=r_mx)
    r_q = region(4 * TOK * 4)
    qP = place("qP", [P, NQ, 4, QB], at=r_q)
    qS = place("qS", [P, NSEQ, 4, LS], at=r_q + NQ * 4 * QB * 4)
    xs = place("xs", [P, XS, D], at=r_q)
    wada_late = place("wada_late", [P, KT, 512], at=r_q)
    wada = [place(f"wada{i}", [P, KT, 512], at=r_h + o * TOK * 4) for i, o in enumerate((0, KT, KT // 2, KT + KT // 2))]
    r_a = top[0]
    Vc = place("Vc", [P, NQ, P])
    r_p = top[0]
    assert r_q + XS * D * 4 <= r_p
    Pb = place("Pb", [P, 2, 4, 192])
    PT1 = place("PT1", [P, 512])
    PT2 = place("PT2", [P, 512])
    vT = place("vT", [P, TOK], at=r_p)
    r_k = top[0]
    kT = place("kT", [P, TOK])
    th = place("th", [P, 2, CW])
    Ks = place("Ks", [P, KVS, 2, WIN])
    Vs = place("Vs", [P, KVS, 2, P])
    r_u = region(3 * UB * 4)
    rt1 = place("rt1", [P, 2, CW], at=r_u)
    rt2 = place("rt2", [P, 2, CW], at=r_u + 2 * CW * 4)
    cosT = place("cosT", [P, TOK], at=r_u + 4 * CW * 4)
    sinT = place("sinT", [P, TOK], at=r_u + 4 * CW * 4 + TOK * 4)
    assert 4 * CW * 4 + 2 * TOK * 4 <= 3 * UB * 4
    uext = place("uext", [P, UW], at=r_u)
    sA = place("sA", [P, UW], at=r_u + UB * 4)
    sB = place("sB", [P, UW], at=r_u + 2 * UB * 4)
    gateB = place("gateB", [P, 2, D], at=r_u)
    w_raw = place("w_raw", [P, RAW, KT, P])
    r_raw = top[0] - RAW * D * 4
    wo_raw = place("wo_raw", [P, RAW, D], at=r_raw)
    xf = place("xf", [P, 2, D], at=r_raw)
    yr = place("yr", [P, 2, D], at=r_raw + 2 * D * 4)
    lnG = place("lnG", [P, D], at=r_h + KT * D * 4)
    lnB = place("lnB", [P, D], at=r_h + (KT * TOK + KT * D) * 4)
    assert KT * (TOK - D) >= D
    r_hl = region(4 * KT * P * 4)
    w_hi = place("w_hi", [P, 2, KT, P], F32R, at=r_hl)
    w_lo = place("w_lo", [P, 2, KT, P], F32R, at=r_hl + 2 * KT * P * 4)
    m_hi = place("m_hi", [P, 2, KT, P], F32R, at=r_hl)
    m_lo = place("m_lo", [P, 2, KT, P], F32R, at=r_hl + 2 * KT * P * 4)
    part = place("part", [P, 2, 512])
    wp = place("wp", [P, 4, P])
    vnew = place("vnew", [LS, NSEQ, P])
    ident = place("ident", [P, P])
    sel = place("sel", [P, 9])
    ebc = place("ebc", [P, 2, P])
    cT = place("cT", [P, KT, 9])
    thc = place("thc", [P, KT, 9])
    cpad = place("cpad", [P, KT, 32])
    bT = place("bT", [P, 24])
    shT = place("shT", [P, KT, 9])
    s1T = place("s1T", [P, KT, 9])
    psc = place("psc", [P, 4])
    psc2 = place("psc2", [P, 4])
    nsp = place("nsp", [P, 4])
    nss = place("nss", [P, 2])
    skp = place("skp", [P, 4])
    sks = place("sks", [P, 2])
    bnst = place("bnst", [P, 2, 12])
    mv = place("mv", [P, 2, 2])
    veps = place("veps", [P, 2 * TILES])
    nmu = place("nmu", [P, 2 * TILES])
    rstd = place("rstd", [P, 2 * TILES])
    nmr = place("nmr", [P, 2 * TILES])
    mhalf = place("mhalf", [P, 1])
    mxs = place("mxs", [P, 2, 4])
    negm = place("negm", [P, 2, 4])
    sdl = place("sdl", [P, 2, 4])
    es = place("es", [P, 2, 4])
    rs = place("rs", [P, 2, 4])
    den = place("den", [P, 2, 4])
    rden = place("rden", [P, 2, 4])
    invc = place("invc", [P, HIST])
    fix = place("fix", [P, HIST])

    proj_ps = nc.alloc_psum_tensor("proj_ps", [P, 3, 512], F32)
    s_ps = nc.alloc_psum_tensor("s_ps", [P, 2, 512], F32)
    t_ps = nc.alloc_psum_tensor("t_ps", [P, 2, 512], F32)
    o_ps = nc.alloc_psum_tensor("o_ps", [P, 512], F32)

    sem = nc.alloc_semaphore
    ld_c = sem("ld_c"); ld_id = sem("ld_id"); ld_small = sem("ld_small"); ld_cs = sem("ld_cs"); ld_brow = sem("ld_brow")
    ld_ada = [sem(f"ld_ada{i}") for i in range(4)]
    ld_late = sem("ld_late")
    ld_x = [sem(f"ld_x{i}") for i in range(XS)]
    ld_w = [sem(f"ld_w{i}") for i in range(RAW)]
    ld_kv = [sem(f"ld_kv{i}") for i in range(KVS)]
    ld_hist = sem("ld_hist"); ld_ln = sem("ld_ln")
    ld_xf = [sem(f"ld_xf{i}") for i in range(2)]
    st_y = [sem(f"st_y{i}") for i in range(2)]
    st_u = sem("st_u"); st_misc = sem("st_misc"); st_k = sem("st_k"); st_v = sem("st_v")
    ada_done = sem("ada_done"); sel_done = sem("sel_done"); xt_done = sem("xt_done"); unit_done = sem("unit_done")
    vt_done = sem("vt_done"); s_done = sem("s_done"); t_done = sem("t_done"); pv_done = sem("pv_done"); y_done = sem("y_done")
    thc_done = sem("thc_done"); xn_done = sem("xn_done"); ada_evac = sem("ada_evac"); xte_a = sem("xte_a")
    hhi_done = sem("hhi_done"); whi_done = sem("whi_done"); act_free = sem("act_free"); th_done = sem("th_done")
    exp_done = sem("exp_done"); es_done = sem("es_done"); pt1_done = sem("pt1_done"); mhi_done = sem("mhi_done"); yn_done = sem("yn_done")
    dve_step = sem("dve_step"); c_done = sem("c_done"); stats_done = sem("stats_done"); xte_v = sem("xte_v"); mod_done = sem("mod_done")
    hx_done = sem("hx_done"); hlo_v = sem("hlo_v"); dve_free = sem("dve_free"); rope_done = sem("rope_done"); mg_done = sem("mg_done")
    d_done = sem("d_done"); max_done = sem("max_done"); p_done = sem("p_done"); pt2_done = sem("pt2_done"); mix_done = sem("mix_done")
    vte_done = sem("vte_done"); mlo_v = sem("mlo_v"); mlo_p = sem("mlo_p"); r_done = sem("r_done"); g_done = sem("g_done"); wlo_v = sem("wlo_v"); consts_v = sem("consts_v")
    pool_step = sem("pool_step"); rstd_done = sem("rstd_done"); wlo_done = sem("wlo_done"); hlo_p = sem("hlo_p"); sum_done = sem("sum_done")
    yb_done = sem("yb_done")

    def cols(c):
        return slice(CW * c, CW * (c + 1))

    block = nc.Block()
    with block as block:

        @block.sync
        def _(sp):
            sp.dma_start(cT[:], cT_d).then_inc(ld_c, 16)

            def load_ada(a):
                sp.dma_start(wada[a][:], w_ada[ADA[a]]).then_inc(ld_ada[a], 16)

            def load_x(t):
                if t >= XS:
                    sp.wait_ge(xt_done, 2 * (t - XS + 1))
                sp.dma_start(xs[:, t % XS, :], x_all[t]).then_inc(ld_x[t % XS], 16)

            def load_w(b):
                if b >= RAW:
                    sp.wait_ge(whi_done, b - RAW + 1)
                    sp.wait_ge(wlo_done, b - RAW + 1)
                sp.dma_start(w_raw[:, b % RAW], w_in[b]).then_inc(ld_w[b % RAW], 16)

            def load_w_out(k):
                b = NBLK + k
                sp.wait_ge(whi_done, b - RAW + 1)
                if k < RAW:
                    sp.wait_ge(wlo_done, b - RAW + 1)
                elif k % 2 == 0:
                    sp.wait_ge(wlo_v, (k - RAW) // 2 + 1)
                else:
                    sp.wait_ge(wlo_done, NBLK + (k - RAW) // 2 + 1)
                sp.dma_start(wo_raw[:, b % RAW], w_out[k]).then_inc(ld_w[b % RAW], 16)

            def load_kv(p):
                pair = slice(2 * p, 2 * p + 2)
                sp.dma_start(Ks[:, p], kcT[pair].rearrange("s p t -> p s t")).then_inc(ld_kv[p], 16)
                sp.dma_start(Vs[:, p], vc[pair].rearrange("s p d -> p s d")).then_inc(ld_kv[p], 16)

            def samples_u():
                return uext[:, UE:UW].rearrange("p (s t) -> p s t", t=HIST + LS)

            def load_history(s):
                if s == 0:
                    sp.wait_ge(rope_done, 15)
                else:
                    sp.wait_ge(d_done, s)
                    sp.wait_ge(st_u, 32 * s)
                sp.dma_start(samples_u()[:, :, 0:HIST], histT[GROUPS[s]]).then_inc(ld_hist, 16)

            def store_u(s):
                g = GROUPS[s]
                sp.wait_ge(act_free, freed_count(unit_index("u", g, NCH - 1))[1])
                sp.dma_start(upT_out[g], uext[:, UE - HIST:UE]).then_inc(st_u, 16)
                sp.dma_start(usT_out[g], samples_u()[:, :, LS:HIST + LS]).then_inc(st_u, 16)

            load_ada(0)
            load_x(0)
            sp.dma_start(ident[:], ident_d).then_inc(ld_id, 16)
            sp.dma_start(sel[:], sel_d).then_inc(ld_id, 16)
            sp.dma_start(bT[:], bT_d).then_inc(ld_id, 16)
            load_x(1)
            load_x(2)
            load_ada(1)
            load_w(0)
            load_w(1)
            load_ada(2)
            load_ada(3)
            load_x(3)
            load_x(4)
            load_x(5)
            sp.dma_start(cosT[:], cos_d).then_inc(ld_cs, 16)
            sp.dma_start(sinT[:], sin_d).then_inc(ld_cs, 16)
            load_x(6)
            load_x(7)
            load_x(8)
            load_w(2)
            sp.dma_start(ebc[:], ebc_d).then_inc(ld_small, 16)
            sp.dma_start(wp[:], w_pool).then_inc(ld_small, 16)
            sp.dma_start(psc[:], pscale_d).then_inc(ld_small, 16)
            sp.dma_start(skp[:], sinkp_d).then_inc(ld_small, 16)
            sp.dma_start(sks[:], sinks_d).then_inc(ld_small, 16)
            load_w(3)
            sp.wait_ge(xt_done, 2 * TILES)
            sp.dma_start(wada_late[:], w_ada[ADA[4]]).then_inc(ld_late, 16)
            load_w(4)
            sp.wait_ge(ada_done, 5)
            sp.dma_start(wada_late[:], w_ada[ADA[5]]).then_inc(ld_late, 16)
            load_w(5)
            sp.wait_ge(ada_evac, 6)
            sp.dma_start(part[9:10, :, :], brow_d).then_inc(ld_brow, 16)
            load_w(6)
            load_w(7)
            load_w(8)
            sp.wait_ge(rope_done, NCH)
            sp.dma_start(kT_out, kT[:, SEQ - WIN:TOK]).then_inc(st_k, 16)
            sp.wait_ge(act_free, NCH)
            sp.dma_start(vT_out, vT[:, SEQ - WIN:TOK]).then_inc(st_v, 16)
            sp.dma_start(kcT_out, kc_tail).then_inc(st_misc, 16)
            sp.dma_start(vc_out, vc_tail).then_inc(st_misc, 16)
            load_w(9)
            load_w(10)
            load_w(11)
            load_w(12)
            for p in range(KVS):
                load_kv(p)
            load_w(13)
            load_w(14)
            load_history(0)
            load_w(15)
            store_u(0)
            load_w(16)
            load_history(1)
            load_w(17)
            store_u(1)
            load_w_out(0)
            load_history(2)
            load_w_out(1)
            store_u(2)
            load_w_out(2)
            load_history(3)
            load_w_out(3)
            store_u(3)
            for k in range(RAW, KT):
                load_w_out(k)
            sp.wait_ge(unit_done, LAST_PROJ + 1)
            sp.dma_start(lnG[:], ln_g.to_broadcast([P, D])).then_inc(ld_ln, 16)
            sp.dma_start(lnB[:], ln_b.to_broadcast([P, D])).then_inc(ld_ln, 16)
            sp.wait_ge(whi_done, NBLK + KT)
            sp.wait_ge(wlo_v, KT // 2)
            sp.wait_ge(wlo_done, NBLK + KT // 2)
            for t in range(TILES):
                if t >= 2:
                    sp.wait_ge(r_done, 2 * (t - 1))
                sp.dma_start(xf[:, t % 2, :], x_all[t]).then_inc(ld_xf[t % 2], 16)
                if t >= 1:
                    sp.wait_ge(yb_done, t)
                    sp.dma_start(y_out[t - 1], yr[:, (t - 1) % 2, :]).then_inc(st_y[(t - 1) % 2], 16)
            last = TILES - 1
            for half in range(2):
                w = slice(512 * half, 512 * (half + 1))
                sp.wait_ge(yb_done, TILES + half)
                sp.dma_start(y_out[last][:, w], yr[:, last % 2, w]).then_inc(st_y[last % 2], 16)
            sp.wait_ge(st_y[0], 16 * (TILES // 2 + 2))
            sp.wait_ge(st_y[1], 16 * (TILES // 2))
            sp.wait_ge(st_k, 16)
            sp.wait_ge(st_v, 16)
            sp.wait_ge(st_u, 32 * 4)
            sp.wait_ge(st_misc, 16 * 2)

        @block.tensor
        def _(pe):
            def ada(a):
                if a < 4:
                    w = wada[a]
                    pe.wait_ge(ld_ada[a], 16)
                else:
                    w = wada_late
                    pe.wait_ge(ld_late, 16 * (a - 3))
                if a == 0:
                    pe.wait_ge(c_done, 1)
                if a >= 2:
                    pe.wait_ge(ada_evac, a - 1)
                for k in range(KT):
                    g = 32 * (k % 4)
                    mm = pe.matmul(s_ps[g:g + 32, a % 2, :], cpad[:, k, :], w[:, k, :], start=(k < 4), stop=(k >= 4), tile_position=(0, g))
                mm.then_inc(ada_done, 1)

            def select(a):
                pe.wait_ge(ada_evac, a + 1)
                if a:
                    pe.wait_ge(mod_done, a)
                for m in range(4):
                    mm = pe.matmul(o_ps[:, 9 * m:9 * m + 9], part[:, a % 2, P * m:P * (m + 1)], sel[:], start=True, stop=True)
                mm.then_inc(sel_done, 1)

            def x_transpose(t):
                pe.wait_ge(xn_done, t + 1)
                if t == 0:
                    pe.wait_ge(ld_id, 48)
                for h in range(2):
                    if t:
                        pe.wait_ge(xte_a if h else xte_v, t)
                    for k in range(4):
                        mm = pe.transpose(t_ps[:, h, P * k:P * (k + 1)], xs[:, t % XS, P * (4 * h + k):P * (4 * h + k + 1)], ident[:])
                    mm.then_inc(xt_done, 1)

            def wait_bank(n):
                if n >= 3:
                    act, v = freed_count(n - 3)
                    pe.wait_ge(act_free if act else dve_free, v)

            def unit(n, slices=range(KT)):
                kind, j, c = UNITS[n]
                bank = proj_ps[:, n % 3, :]
                if slices[0] == 0:
                    wait_bank(n)
                if kind == "z":
                    pe.wait_ge(d_done, GROUPS.index(j) + 1)
                    pe.wait_ge(ld_small, 80)
                    dd = sB if j % 2 == 0 else sA
                    mm = pe.matmul(bank[:, 0:CW], wp[:, j, :], dd[:, cols(c)], start=True, stop=True)
                elif kind == "r":
                    pe.wait_ge(ld_brow, 16)
                    mm = pe.matmul(bank[:], ebc[:, j, :], part[:, c, :], start=True, stop=True)
                else:
                    b = block_of(n)
                    w = b % 2
                    if n == FIRST_UNIT[b] and slices[0] == 0:
                        pe.wait_ge(whi_done, b + 1)
                        pe.wait_ge(wlo_done, b + 1)
                    if kind == "k":
                        for k in slices:
                            if k % 2 == 0:
                                pe.wait_ge(hhi_done, 4 * c + k // 2 + 1)
                            pe.matmul(bank[:, 0:CW], w_hi[:, w, k, :], h_hi[:, k, cols(c)], start=(k == 0), stop=False)
                            pe.matmul(bank[:, 0:CW], w_lo[:, w, k, :], h_hi[:, k, cols(c)], start=False, stop=False)
                        for k in slices:
                            if k % 2 == 0:
                                g = 4 * c + k // 2
                                pe.wait_ge(hlo_p if g % 2 else hlo_v, g // 2 + 1)
                            mm = pe.matmul(bank[:, 0:CW], w_hi[:, w, k, :], h_lo[:, k, cols(c)], start=False, stop=(k == KT - 1))
                    else:
                        for k in slices:
                            hi, lo = h_hi[:, k, cols(c)], h_lo[:, k, cols(c)]
                            pe.matmul(bank[:, 0:CW], w_hi[:, w, k, :], hi, start=(k == 0), stop=False)
                            pe.matmul(bank[:, 0:CW], w_hi[:, w, k, :], lo, start=False, stop=False)
                            mm = pe.matmul(bank[:, 0:CW], w_lo[:, w, k, :], hi, start=False, stop=(k == KT - 1))
                if slices[-1] == KT - 1:
                    mm.then_inc(unit_done, 1)

            def v_transposes(m):
                pe.wait_ge(vte_done, m - 1) if m >= 2 else pe.wait_ge(xte_a if m else xte_v, TILES)
                if m == 0:
                    pe.wait_ge(act_free, NCH)
                for i in range(4):
                    if m < 4:
                        c = 4 * m + i
                        w = P if c < NQ - 1 else QB
                        mm = pe.transpose(t_ps[0:w, m % 2, P * i:P * (i + 1)], vT[:, QB * c:QB * c + w], ident[:])
                    else:
                        s = 4 * (m - 4) + i
                        mm = pe.transpose(t_ps[0:LS, m % 2, P * i:P * (i + 1)], vT[:, SEQ + LS * s:SEQ + LS * (s + 1)], ident[:])
                mm.then_inc(vt_done, 1)

            def scores(i):
                pe.wait_ge(rope_done, NCH + 3 * NCH + min(QB * i // CW, NCH - 1) + 1)
                if i == 0:
                    pe.wait_ge(ada_evac, 6)
                else:
                    pe.wait_ge(exp_done, i)
                for kv in range(2):
                    r = slice(HD * kv, HD * (kv + 1))
                    if i < NQ:
                        nk = sum(keys_of(i))
                        k0 = QB * (i + 1) - nk
                        for p in range(2):
                            mm = pe.matmul(s_ps[:, kv, 192 * p:192 * p + nk], qP[r, i, 2 * p:2 * p + 2, :],
                                           kT[r, k0:k0 + nk], start=True, stop=True, tile_position=(HD * kv, 0))
                    else:
                        sp_ = i - NQ
                        if kv == 0:
                            pe.wait_ge(ld_kv[sp_], 32)
                        for e in range(2):
                            t0 = SEQ + LS * (2 * sp_ + e)
                            q = qS[r, 2 * sp_ + e, :, :]
                            o = s_ps[HD * e:HD * (e + 1), kv, :]
                            pe.matmul(o[:, 0:WIN], q, Ks[r, sp_, e, :], start=True, stop=True, tile_position=(HD * kv, HD * e))
                            mm = pe.matmul(o[:, WIN:WIN + LS], q, kT[r, t0:t0 + LS], start=True, stop=True, tile_position=(HD * kv, HD * e))
                mm.then_inc(s_done, 1)

            def p_transposes(i):
                pe.wait_ge(p_done, i + 1)
                if i:
                    pe.wait_ge(pt1_done, i)
                    if seconds(i - 1):
                        pe.wait_ge(pt2_done, seconds(i - 1))
                else:
                    pe.wait_ge(vte_done, 6)
                k1, k2 = keys_of(i)
                for j in range(4 if i < NQ else 2):
                    mm = pe.transpose(t_ps[0:k1, 0, P * j:P * (j + 1)], Pb[:, i % 2, j, 0:k1], ident[:])
                    if k2:
                        mm = pe.transpose(t_ps[0:k2, 1, P * j:P * (j + 1)], Pb[:, i % 2, j, WIN:WIN + k2], ident[:])
                mm.then_inc(t_done, 1)

            def values(i):
                pe.wait_ge(pt1_done, i + 1)
                if seconds(i):
                    pe.wait_ge(pt2_done, seconds(i))
                if i:
                    pe.wait_ge(mix_done, i)
                k1, k2 = keys_of(i)
                for kv in range(2):
                    d = slice(HD * kv, HD * (kv + 1))
                    if i < NQ:
                        o = o_ps[d, 0:256]
                        mm = pe.matmul(o, Vc[0:k1, max(i - 2, 0), d], PT1[0:k1, 256 * kv:256 * (kv + 1)], start=True, stop=not k2,
                                       tile_position=(0, HD * kv))
                        if k2:
                            mm = pe.matmul(o, Vc[0:QB, i, d], PT2[0:QB, 256 * kv:256 * (kv + 1)], start=False, stop=True,
                                           tile_position=(0, HD * kv))
                    else:
                        sp_ = i - NQ
                        for e in range(2):
                            o = o_ps[d, HD * e:HD * (e + 1)]
                            w = slice(P * kv + HD * e, P * kv + HD * (e + 1))
                            pe.matmul(o, Vs[:, sp_, e, d], PT1[:, w], start=True, stop=False, tile_position=(0, HD * kv))
                            mm = pe.matmul(o, vnew[0:LS, 2 * sp_ + e, d], PT2[0:LS, w], start=False, stop=True, tile_position=(0, HD * kv))
                mm.then_inc(pv_done, 1)

            def slot(i):
                if 0 <= i - 2 < NSTEP:
                    values(i - 2)
                if 0 <= i - 1 < NSTEP:
                    p_transposes(i - 1)
                if i < NSTEP:
                    scores(i)

            def output_half(t, halves, k):
                for half in halves:
                    o = proj_ps[:, (NU + 2 * t + half) % 3, :]
                    w = slice(512 * half, 512 * (half + 1))
                    pe.matmul(o, m_hi[:, t % 2, k, :], wo_hi[:, k, w], start=(k == 0), stop=False)
                    pe.matmul(o, m_hi[:, t % 2, k, :], wo_lo[:, k, w], start=False, stop=False)
                    mm = pe.matmul(o, m_lo[:, t % 2, k, :], wo_hi[:, k, w], start=False, stop=(k == KT - 1))
                    if k == KT - 1:
                        mm.then_inc(y_done, 1)

            low, high = range(KT // 2), range(KT // 2, KT)
            ada(0)
            x_transpose(0)
            x_transpose(1)
            x_transpose(2)
            ada(1)
            select(0)
            select(1)
            unit(0, low)
            unit(1, low)
            ada(2)
            select(2)
            ada(3)
            select(3)
            x_transpose(3)
            unit(0, high)
            x_transpose(4)
            unit(1, high)
            x_transpose(5)
            after = {2: [(x_transpose, 6), (x_transpose, 7), (x_transpose, 8)],
                     6: [(v_transposes, 0), (v_transposes, 1)], 7: [(ada, 4), (v_transposes, 2), (v_transposes, 3)],
                     8: [(v_transposes, 4), (v_transposes, 5)], 11: [(ada, 5)]}
            for n in range(2, NU):
                unit(n)
                for f, a in after.get(n, []):
                    f(a)
                for i in SLOTS.get(n, []):
                    slot(i)
            for t in range(TILES):
                pe.wait_ge(mhi_done, t + 1)
                if t == 0:
                    pe.wait_ge(mlo_v, 1)
                    wait_bank(NU)
                    wait_bank(NU + 1)
                    for k in range(KT):
                        pe.wait_ge(whi_done, NBLK + k + 1)
                        pe.wait_ge(wlo_v if k % 2 == 0 else wlo_done, (0 if k % 2 == 0 else NBLK) + k // 2 + 1)
                        output_half(0, (0, 1), k)
                    for i in SLOTS.get(NU, []) + SLOTS.get(NU + 1, []):
                        slot(i)
                    continue
                pe.wait_ge(mlo_p, t)
                for half in range(2):
                    m = 2 * t + half
                    if m < 3:
                        wait_bank(NU + m)
                    else:
                        pe.wait_ge(g_done, m - 2)
                    for k in range(KT):
                        output_half(t, (half,), k)
                    for i in SLOTS.get(NU + m, []):
                        slot(i)

        @block.scalar
        def _(act):
            def normalise(t):
                act.wait_ge(rstd_done, t + 1)
                act.activation(xs[:, t % XS, :], xs[:, t % XS, :], ACT.Identity, bias=nmr[:, t:t + 1], scale=rstd[:, t:t + 1]).then_inc(xn_done, 1)

            def evac_ada(a):
                act.wait_ge(ada_done, a + 1)
                if a >= 2:
                    act.wait_ge(sel_done, min(a - 1, 4))
                act.activation(part[:, a % 2, :], s_ps[:, a % 2, :], ACT.Identity, scale=0.5).then_inc(ada_evac, 1)

            def evac_xt(t):
                act.wait_ge(xt_done, 2 * t + 2)
                act.activation(xnT[:, 4:8, P * t:P * (t + 1)], t_ps[:, 1, :].rearrange("p (k t) -> p k t", t=P), ACT.Copy).then_inc(xte_a, 1)

            def h_high(c, groups=range(4)):
                for g in groups:
                    act.wait_ge(hx_done, 4 * c + g + 1)
                    act.activation(h_hi[:, 2 * g:2 * g + 2, cols(c)], xnT[:, 2 * g:2 * g + 2, cols(c)], ACT.Copy).then_inc(hhi_done, 1)

            def w_high(b):
                act.wait_ge(ld_w[b % RAW], 16 * (b // RAW + 1))
                if b >= 2:
                    act.wait_ge(unit_done, LAST_UNIT[b - 2] + 1)
                act.activation(w_hi[:, b % 2], w_raw[:, b % RAW], ACT.Copy).then_inc(whi_done, 1)

            def evac_unit(n):
                kind, j, c = UNITS[n]
                src = proj_ps[:, n % 3, 0:CW]
                if kind in ("k", "q", "z"):
                    return
                act.wait_ge(unit_done, n + 1)
                if kind == "v":
                    act.activation(vT[:, cols(c)], src, ACT.Copy).then_inc(act_free, 1)
                elif kind in ("ga", "gp"):
                    i = GATES.index(n)
                    if i >= 2:
                        act.wait_ge(dve_free, freed_count(GATES[i - 2])[1])
                    act.activation(th[:, i % 2, :], src, ACT.Tanh, scale=0.5).then_inc(th_done, 1)
                elif kind == "u":
                    if c == 0:
                        s = GROUPS.index(j)
                        if s == 0:
                            act.wait_ge(rope_done, 15)
                        else:
                            act.wait_ge(d_done, s)
                            act.wait_ge(st_u, 32 * s)
                    if c < 2:
                        act.activation(uext[:, HIST + CW * c:HIST + CW * (c + 1)], src, ACT.Copy).then_inc(act_free, 1)
                    else:
                        act.activation(uext[:, HIST + 2 * CW:UE], src[:, 0:PW2], ACT.Copy)
                        act.activation(uext[:, UE:UW].rearrange("p (s t) -> p s t", t=HIST + LS)[:, :, HIST:],
                                       src[:, PW2:CW].rearrange("p (s t) -> p s t", t=LS), ACT.Copy).then_inc(act_free, 1)
                else:
                    if j == 0 and c == 0:
                        act.wait_ge(d_done, 4)
                        act.wait_ge(st_u, 32 * 4)
                    act.activation(gateB[:, j, 512 * c:512 * (c + 1)], proj_ps[:, n % 3, :], ACT.Copy).then_inc(act_free, 1)

            def slot(i):
                if 0 <= i - 1 < NSTEP:
                    k1, _ = keys_of(i - 1)
                    w = 512 if i - 1 < NQ else 256
                    act.wait_ge(t_done, i)
                    if i >= 2:
                        act.wait_ge(pv_done, i - 1)
                    act.activation(PT1[0:k1, 0:w], t_ps[0:k1, 0, 0:w], ACT.Copy).then_inc(pt1_done, 1)
                if i < NSTEP:
                    act.wait_ge(max_done, i + 1)
                    if i == 0:
                        act.wait_ge(st_v, 16)
                    if i >= 2:
                        act.wait_ge(t_done, i - 1)
                        act.wait_ge(p_done, i - 1)
                    nj, nk = (4 if i < NQ else 2), sum(keys_of(i))
                    act.activation(es[:, i % 2, 0:nj], sdl[:, i % 2, 0:nj], ACT.Exp).then_inc(es_done, 1)
                    for j in range(nj):
                        src = s_ps[:, j // 2, 192 * (j % 2):192 * (j % 2) + nk] if i < NQ else s_ps[:, j, 0:nk]
                        e = act.activation(Pb[:, i % 2, j, 0:nk], src, ACT.Exp, bias=negm[:, i % 2, j:j + 1], scale=SCALE,
                                           accum_out=rs[:, i % 2, j:j + 1])
                    e.then_inc(exp_done, 1)

            def wo_high(k):
                i = NBLK + k
                act.wait_ge(ld_w[i % RAW], 16 * (i // RAW + 1))
                act.activation(wo_hi[:, k, :], wo_raw[:, i % RAW, :], ACT.Copy).then_inc(whi_done, 1)

            def mixed_high(t):
                act.wait_ge(mix_done, 2 * t + 2 if t < TILES - 1 else NSTEP)
                act.wait_ge(dve_free, freed_count(unit_index("z", GROUPS[3], t // 3))[1])
                if t >= 2:
                    act.wait_ge(y_done, 2 * (t - 1))
                act.activation(m_hi[:, t % 2], mixed[:, :, P * t:P * (t + 1)], ACT.Copy).then_inc(mhi_done, 1)

            act.wait_ge(ld_c, 16)
            act.activation(thc[:], cT[:], ACT.Tanh, scale=0.5).then_inc(thc_done, 1)
            normalise(0)
            evac_ada(0)
            normalise(1)
            evac_xt(0)
            normalise(2)
            evac_xt(1)
            evac_xt(2)
            evac_ada(1)
            w_high(0)
            h_high(0, (0, 1))
            w_high(1)
            evac_ada(2)
            evac_ada(3)
            normalise(3)
            h_high(0, (2, 3))
            evac_xt(3)
            normalise(4)
            normalise(5)
            evac_xt(4)
            evac_xt(5)
            h_high(1)
            evac_unit(1)
            normalise(6)
            normalise(7)
            evac_xt(6)
            normalise(8)
            evac_xt(7)
            evac_xt(8)
            evac_unit(3)
            h_high(2)
            w_high(2)
            evac_unit(5)
            w_high(3)
            after = {7: 4, 11: 5}
            for n in range(6, NU):
                b = block_of(n)
                evac_unit(n)
                if n in after:
                    evac_ada(after[n])
                for i in SLOTS.get(n, []):
                    slot(i)
                if b is not None and LAST_UNIT[b] == n and b + 2 < NBLK:
                    w_high(b + 2)
            act.wait_ge(unit_done, LAST_PROJ + 1)
            wo_high(0)
            mixed_high(0)
            for k in range(1, KT):
                wo_high(k)
            mixed_high(1)
            for m in range(2 * TILES):
                if m % 2 == 0 and 2 <= m // 2 + 1 < TILES:
                    mixed_high(m // 2 + 1)
                for i in SLOTS.get(NU + m, []):
                    slot(i)

        @block.vector
        def _(dve):
            steps = [0]

            def link(ins):
                steps[0] += 1
                ins.then_inc(dve_step, 1)
                dve.wait_ge(dve_step, steps[0])

            def stats(t, src):
                b = t % 2
                dve.bn_stats(bnst[:, b, 0:6], src[:, 0:512])
                link(dve.bn_stats(bnst[:, b, 6:12], src[:, 512:1024]))
                mean_var(t)

            def mean_var(t):
                b = t % 2
                link(dve.bn_aggr(mv[:, b, :], bnst[:, b, :]))
                dve.tensor_scalar(nmu[:, t:t + 1], mv[:, b, 0:1], -1.0, None, ALU.mult)
                dve.tensor_scalar(veps[:, t:t + 1], mv[:, b, 1:2], EPS, None, ALU.add).then_inc(stats_done, 1)

            def x_stats(t):
                dve.wait_ge(ld_x[t % XS], 16 * (t // XS + 1))
                stats(t, xs[:, t % XS, :])

            def evac_xt(t):
                dve.wait_ge(xt_done, 2 * t + 1)
                dve.tensor_copy(xnT[:, 0:4, P * t:P * (t + 1)], t_ps[:, 0, :].rearrange("p (k t) -> p k t", t=P)).then_inc(xte_v, 1)

            def modulation(a):
                dve.wait_ge(sel_done, a + 1)
                if a == 0:
                    dve.wait_ge(ld_id, 48)
                ci = ADA[a]
                dst = shT if ci < 2 else s1T
                k0 = 4 * (ci % 2)
                dve.scalar_tensor_tensor(dst[:, k0:k0 + 4, :], o_ps[:, 0:36].rearrange("p (k s) -> p k s", s=9), 0.0 if ci < 2 else 1.0,
                                         bT[:, 4 * ci:4 * ci + 4].unsqueeze(2).to_broadcast([P, 4, 9]), ALU.add, ALU.add).then_inc(mod_done, 1)

            def h_chunk(c, groups=range(4)):
                dve.wait_ge(mod_done, groups[-1] + 1 if c == 0 else 4)
                dve.wait_ge(xte_a, 3 * c + 3)
                dve.wait_ge(xte_v, 3 * c + 3)
                pw = CW if c < 2 else PW2
                if c == 2:
                    v = xnT[:, :, SEQ:TOK].rearrange("p k (s t) -> p k s t", t=LS)
                    for src, op in ((s1T, ALU.mult), (shT, ALU.add)):
                        link(dve.tensor_tensor(v, v, src[:, :, 1:9].unsqueeze(3).to_broadcast([P, KT, NSEQ, LS]), op))
                for g in groups:
                    for k in (2 * g, 2 * g + 1):
                        x = xnT[:, k, CW * c:CW * c + pw]
                        last = dve.tensor_scalar(x, x, s1T[:, k, 0:1], shT[:, k, 0:1], ALU.mult, ALU.add)
                    last.then_inc(hx_done, 1)
                for g in groups:
                    if g % 2 == 0:
                        dve.wait_ge(hhi_done, 4 * c + g + 1)
                        w = slice(2 * g, 2 * g + 2)
                        dve.tensor_tensor(h_lo[:, w, cols(c)], xnT[:, w, cols(c)], h_hi[:, w, cols(c)].bitcast(F32), ALU.subtract).then_inc(hlo_v, 1)

            def evac_unit(n):
                kind, j, c = UNITS[n]
                src = proj_ps[:, n % 3, 0:CW]
                if kind in ("v", "u", "r"):
                    return
                if kind in ("k", "q"):
                    i = count(("k", "q"), n) - 1
                    if i == 0:
                        dve.wait_ge(ld_cs, 32)
                    if kind == "q" and j == 0 and c == 0:
                        dve.wait_ge(ada_done, 6)
                    dve.wait_ge(unit_done, n + 1)
                    r = i % 2
                    dve.stream_shuffle(rt1[:, r, :], src, [(m + 16) % 32 for m in range(32)])
                    dve.tensor_tensor(rt2[:, r, :], src, cosT[:, cols(c)], ALU.mult).then_inc(dve_free, 1)
                    dve.wait_ge(dve_free, freed_count(n)[1])
                    link(dve.tensor_tensor(rt1[:, r, :], rt1[:, r, :], sinT[:, cols(c)], ALU.mult))
                    if kind == "k":
                        dve.tensor_tensor(kT[:, cols(c)], rt1[:, r, :], rt2[:, r, :], ALU.add).then_inc(rope_done, 1)
                        return
                    pw = CW if c < 2 else PW2
                    nq = CW // QB
                    a, b = (x[:, r, 0:pw].rearrange("p (q t) -> p q t", t=QB) for x in (rt1, rt2))
                    last = dve.tensor_tensor(qP[:, nq * c:nq * c + pw // QB, j, :], a, b, ALU.add)
                    if c == 2:
                        a, b = (x[:, r, pw:CW].rearrange("p (s t) -> p s t", t=LS) for x in (rt1, rt2))
                        last = dve.tensor_tensor(qS[:, :, j, :], a, b, ALU.add)
                    last.then_inc(rope_done, 1)
                elif kind in ("ga", "gp"):
                    i = count(("ga", "gp"), n) - 1
                    dve.wait_ge(th_done, i + 1)
                    if n == FIRST_UNIT[GA_BLK[0]]:
                        dve.wait_ge(hlo_p, 6)
                        dve.wait_ge(hhi_done, 12)
                    dst = mixed[:, j if kind == "ga" else 4 + j, cols(c)]
                    dve.scalar_tensor_tensor(dst, th[:, i % 2, :], 1.0, src, ALU.add, ALU.mult).then_inc(dve_free, 1)
                else:
                    dve.wait_ge(unit_done, n + 1)
                    dve.wait_ge(dve_free, freed_count(unit_index("gp", j, c))[1])
                    dst = mixed[:, 4 + j, cols(c)]
                    dve.scalar_tensor_tensor(dst, src, psc2[:, j:j + 1], dst, ALU.mult, ALU.mult).then_inc(dve_free, 1)

            def pool_mean(g):
                w = 2 << g
                s, d = (sA, sB) if g % 2 == 0 else (sB, sA)
                dve.wait_ge(sum_done, GROUPS.index(g) + 1)
                link(dve.tensor_tensor(fix[:, 0:w - 1], s[:, HIST:HIST + w - 1], invc[:, 0:w - 1], ALU.mult))
                dve.scalar_tensor_tensor(d[:, w - 1:SEQ], s[:, HIST + w - 1:UE], 1.0 / w, uext[:, HIST + w - 1:UE], ALU.mult, ALU.subtract)
                dve.tensor_tensor(d[:, 0:w - 1], fix[:, 0:w - 1], uext[:, HIST:HIST + w - 1], ALU.subtract)

                def samples(x):
                    return x[:, UE:UW].rearrange("p (s t) -> p s t", t=HIST + LS)[:, :, HIST:]

                dve.scalar_tensor_tensor(d[:, SEQ:TOK].rearrange("p (s t) -> p s t", t=LS), samples(s), 1.0 / w, samples(uext),
                                         ALU.mult, ALU.subtract).then_inc(d_done, 1)

            def evac_v(m):
                dve.wait_ge(vt_done, m + 1)
                if m < 4:
                    if m < 3:
                        dve.tensor_copy(Vc[:, 4 * m:4 * m + 4, :], t_ps[:, m % 2, :].rearrange("p (c d) -> p c d", d=P)).then_inc(vte_done, 1)
                    else:
                        dve.tensor_copy(Vc[:, 12:15, :], t_ps[:, 1, 0:3 * P].rearrange("p (c d) -> p c d", d=P))
                        dve.tensor_copy(Vc[0:QB, 15, :], t_ps[0:QB, 1, 3 * P:4 * P]).then_inc(vte_done, 1)
                else:
                    dve.tensor_copy(vnew[:, 4 * (m - 4):4 * (m - 3), :], t_ps[0:LS, m % 2, :].rearrange("p (c d) -> p c d", d=P)).then_inc(vte_done, 1)

            def mix(i):
                dve.wait_ge(pv_done, i + 1)
                if i < NQ:
                    g = mixed[:, 0:4, QB * i:QB * (i + 1)]
                    dve.scalar_tensor_tensor(g, o_ps[:, 0:256].rearrange("p (j t) -> p j t", t=QB), 0.5, g, ALU.mult, ALU.mult).then_inc(mix_done, 1)
                else:
                    for e in range(2):
                        t0 = SEQ + LS * (2 * (i - NQ) + e)
                        g = mixed[:, 0:4, t0:t0 + LS]
                        last = dve.scalar_tensor_tensor(g, o_ps[:, HD * e:HD * (e + 1)].rearrange("p (j t) -> p j t", t=LS), 0.5, g, ALU.mult, ALU.mult)
                    last.then_inc(mix_done, 1)

            def slot(i):
                if 0 <= i - 2 < NSTEP:
                    mix(i - 2)
                if 0 <= i - 1 < NSTEP and keys_of(i - 1)[1]:
                    k2 = keys_of(i - 1)[1]
                    w = 512 if i - 1 < NQ else 256
                    dve.wait_ge(t_done, i)
                    if i >= 2:
                        dve.wait_ge(pv_done, i - 1)
                    dve.tensor_copy(PT2[0:k2, 0:w], t_ps[0:k2, 1, 0:w]).then_inc(pt2_done, 1)
                if i < NSTEP:
                    b, nk = i % 2, sum(keys_of(i))
                    dve.wait_ge(s_done, i + 1)
                    if i < NQ:
                        nj, sink = 4, nsp
                        src = s_ps[:, :, 0:384].rearrange("p b (r n) -> p b r n", n=192)[:, :, :, 0:nk]
                        out = mxs[:, b, :].rearrange("p (b r) -> p b r", r=2)
                    else:
                        nj, sink = 2, nss
                        src, out = s_ps[:, :, 0:nk], mxs[:, b, 0:2]
                    link(dve.tensor_reduce(out, src, AX.X, ALU.max))
                    link(dve.scalar_tensor_tensor(negm[:, b, 0:nj], mxs[:, b, 0:nj], -SCALE, sink[:, 0:nj], ALU.mult, ALU.min))
                    dve.tensor_tensor(sdl[:, b, 0:nj], negm[:, b, 0:nj], sink[:, 0:nj], ALU.subtract).then_inc(max_done, 1)
                    dve.wait_ge(exp_done, i + 1)
                    dve.wait_ge(es_done, i + 1)
                    link(dve.tensor_tensor(den[:, b, 0:nj], rs[:, b, 0:nj], es[:, b, 0:nj], ALU.add))
                    link(dve.reciprocal(rden[:, b, 0:nj], den[:, b, 0:nj]))
                    p = Pb[:, b, 0:nj, 0:nk]
                    dve.tensor_tensor(p, p, rden[:, b, 0:nj].unsqueeze(2).to_broadcast([P, nj, nk]), ALU.mult).then_inc(p_done, 1)

            link(dve.memset(cpad[:], 0.0))
            dve.memset(mhalf[:], -0.5).then_inc(consts_v, 1)
            dve.wait_ge(thc_done, 1)
            dve.scalar_tensor_tensor(cpad[:, :, 0:9], thc[:], 1.0, cT[:], ALU.add, ALU.mult).then_inc(c_done, 1)
            for m in range(HIST):
                last = dve.memset(invc[:, m:m + 1], 1.0 / (m + 1))
            link(last)
            x_stats(0)
            x_stats(1)
            evac_xt(0)
            x_stats(2)
            evac_xt(1)
            evac_xt(2)
            modulation(0)
            modulation(1)
            h_chunk(0, (0, 1))
            modulation(2)
            modulation(3)
            x_stats(3)
            h_chunk(0, (2, 3))
            x_stats(4)
            x_stats(5)
            evac_xt(3)
            evac_xt(4)
            evac_xt(5)
            h_chunk(1)
            evac_unit(0)
            x_stats(6)
            x_stats(7)
            x_stats(8)
            evac_xt(6)
            evac_xt(7)
            evac_xt(8)
            evac_unit(2)
            h_chunk(2)
            evac_unit(4)
            after = {6: [0, 1], 7: [2, 3], 8: [4, 5]}
            for n in range(6, NU):
                if n == 9:
                    dve.wait_ge(ld_small, 16 * 5)
                    dve.tensor_scalar(psc2[:], psc[:], 0.5, None, ALU.mult)
                    dve.tensor_scalar(nsp[:], skp[:], -1.0, None, ALU.mult)
                    link(dve.tensor_scalar(nss[:], sks[:], -1.0, None, ALU.mult))
                kind, j, c = UNITS[n]
                evac_unit(n)
                if kind == "gp" and c == (NCH - 1 if j != GROUPS[3] else 0):
                    pool_mean(j)
                for m in after.get(n, []):
                    evac_v(m)
                for i in SLOTS.get(n, []):
                    slot(i)

            def wo_low(k):
                dve.wait_ge(whi_done, NBLK + k + 1)
                dve.tensor_tensor(wo_lo[:, k, :], wo_raw[:, (NBLK + k) % RAW, :], wo_hi[:, k, :].bitcast(F32), ALU.subtract).then_inc(wlo_v, 1)

            wo_low(0)
            dve.wait_ge(mhi_done, 1)
            dve.tensor_tensor(m_lo[:, 0], mixed[:, :, 0:P], m_hi[:, 0].bitcast(F32), ALU.subtract).then_inc(mlo_v, 1)
            for k in range(2, KT, 2):
                wo_low(k)
            for t in range(TILES):
                row = 0 if t < TILES - 1 else 1
                for half in range(2):
                    m = 2 * t + half
                    w = slice(512 * half, 512 * (half + 1))
                    r = yr[:, t % 2, w]
                    dve.wait_ge(y_done, m + 1)
                    if m == 0:
                        dve.wait_ge(act_free, freed_count(unit_index("r", 1, 1))[1])
                        dve.wait_ge(whi_done, NBLK + KT)
                        dve.wait_ge(wlo_done, NBLK + KT // 2)
                    if t >= 2 and half == 0:
                        dve.wait_ge(st_y[t % 2], 16 * (t // 2))
                    dve.tensor_tensor(r, proj_ps[:, (NU + m) % 3, :], gateB[:, row, w], ALU.mult).then_inc(g_done, 1)
                    dve.wait_ge(g_done, m + 1)
                    dve.wait_ge(ld_xf[t % 2], 16 * (t // 2 + 1))
                    dve.scalar_tensor_tensor(r, xf[:, t % 2, w], ALPHA, r, ALU.mult, ALU.add).then_inc(r_done, 1)
                    dve.wait_ge(r_done, m + 1)
                    last = dve.bn_stats(bnst[:, (TILES + t) % 2, 6 * half:6 * half + 6], r)
                    if half:
                        link(last)
                        mean_var(TILES + t)
                        dve.wait_ge(stats_done, TILES + t + 1)
                        if t == 0:
                            dve.wait_ge(ld_ln, 32)
                        r = yr[:, t % 2, :]
                        link(dve.scalar_tensor_tensor(r, r, nmu[:, TILES + t:TILES + t + 1], lnG[:], ALU.add, ALU.mult))
                        dve.wait_ge(rstd_done, TILES + t + 1)
                        for w in [slice(0, D)] if t < TILES - 1 else [slice(0, 512), slice(512, D)]:
                            dve.scalar_tensor_tensor(r[:, w], r[:, w], rstd[:, TILES + t:TILES + t + 1], lnB[:, w], ALU.mult, ALU.add).then_inc(yb_done, 1)
                    for i in SLOTS.get(NU + m, []):
                        slot(i)

        @block.gpsimd
        def _(pool):
            steps = [0]

            def link(ins):
                steps[0] += 1
                ins.then_inc(pool_step, 1)
                pool.wait_ge(pool_step, steps[0])

            def inv_std(t):
                pool.wait_ge(stats_done, t + 1)
                power = pool.tensor_tensor(rstd[:, t:t + 1], veps[:, t:t + 1], mhalf[:], ALU.pow)
                if t < TILES:
                    link(power)
                    power = pool.tensor_tensor(nmr[:, t:t + 1], nmu[:, t:t + 1], rstd[:, t:t + 1], ALU.mult)
                power.then_inc(rstd_done, 1)

            def w_low(b):
                pool.wait_ge(whi_done, b + 1)
                pool.tensor_tensor(w_lo[:, b % 2], w_raw[:, b % RAW], w_hi[:, b % 2].bitcast(F32), ALU.subtract).then_inc(wlo_done, 1)

            def h_low(c, groups=(1, 3)):
                for g in groups:
                    pool.wait_ge(hhi_done, 4 * c + g + 1)
                    w = slice(2 * g, 2 * g + 2)
                    pool.tensor_tensor(h_lo[:, w, cols(c)], xnT[:, w, cols(c)], h_hi[:, w, cols(c)].bitcast(F32), ALU.subtract).then_inc(hlo_p, 1)

            def window_sums(s, part):
                g = GROUPS[s]
                if s == 0 and part == 0:
                    pool.wait_ge(rope_done, 15)
                    link(pool.memset(uext[:, 0:HIST], 0.0))
                pool.wait_ge(act_free, freed_count(unit_index("u", g, 1 + part))[1])
                if part:
                    pool.wait_ge(ld_hist, 16 * (s + 1))
                elif s:
                    pool.wait_ge(unit_done, unit_index("z", GROUPS[s - 1], NCH - 1) + 1)
                src, lag = uext, 1
                for m in range(g + 1):
                    dst = sA if m % 2 == 0 else sB
                    end = HIST + 2 * CW - (lag - 1)
                    a, b = (end, UW) if part else (2 * lag - 1, end)
                    ins = pool.tensor_tensor(dst[:, a:b], src[:, a:b], src[:, a - lag:b - lag], ALU.add)
                    if m < g or not part:
                        link(ins)
                    src, lag = dst, 2 * lag
                if part:
                    ins.then_inc(sum_done, 1)

            pool.wait_ge(consts_v, 1)
            inv_std(0)
            inv_std(1)
            inv_std(2)
            w_low(0)
            h_low(0, (1,))
            w_low(1)
            inv_std(3)
            h_low(0, (3,))
            inv_std(4)
            inv_std(5)
            h_low(1)
            inv_std(6)
            inv_std(7)
            inv_std(8)
            h_low(2)
            for b in range(2, NBLK):
                s = (b - 12) // 2 if b < NBLK - 1 else 3
                if b >= 12 and (b % 2 == 0):
                    window_sums(s, 0)
                w_low(b)
                if b >= 12 and (b % 2 == 0):
                    window_sums(s, 1)
            window_sums(3, 0)
            window_sums(3, 1)
            for k in range(1, KT, 2):
                pool.wait_ge(whi_done, NBLK + k + 1)
                pool.tensor_tensor(wo_lo[:, k, :], wo_raw[:, (NBLK + k) % RAW, :], wo_hi[:, k, :].bitcast(F32), ALU.subtract).then_inc(wlo_done, 1)
            for t in range(TILES):
                if t + 1 < TILES:
                    pool.wait_ge(mhi_done, t + 2)
                    pool.tensor_tensor(m_lo[:, (t + 1) % 2], mixed[:, :, P * (t + 1):P * (t + 2)], m_hi[:, (t + 1) % 2].bitcast(F32),
                                       ALU.subtract).then_inc(mlo_p, 1)
                inv_std(TILES + t)



def head_dims():
    return np.concatenate([np.r_[16 * q:16 * q + 16, 32 + 16 * q:32 + 16 * q + 16] for q in range(2)])


def projection_columns():
    perm = head_dims()
    pair = [np.r_[HD * j:HD * (j + 1), HD * (4 + j):HD * (5 + j)] for j in range(4)]
    qpair = [np.r_[HD * j + perm, HD * (4 + j) + perm] for j in range(4)]
    k = 512 + np.r_[perm, HD + perm]
    v = 640 + np.arange(P)
    ga = [768 + p for p in pair]
    pooled = [a for g in GROUPS for a in (1280 + P * g + np.arange(P), 1792 + P * g + np.arange(P))]
    return np.concatenate([k, v, *ga, *qpair, *pooled])


def tables():
    pos = np.concatenate([np.arange(SEQ), np.tile(1024 + np.arange(LS), NSEQ)]).astype(np.float32)
    half = HD // 2
    inv = (10000.0 ** (-np.arange(half) / half)).astype(np.float32)
    ang = (inv[:, None] * pos[None, :]).astype(np.float64)
    perm = head_dims()
    rows = np.r_[perm, perm]
    cos = np.cos(ang).astype(np.float32)[rows % half]
    sin = np.sin(ang).astype(np.float32)[rows % half] * np.where(rows < half, -1.0, 1.0).astype(np.float32)[:, None]
    ident = np.eye(P, dtype=np.float32)
    sel = np.zeros((P, 9), np.float32)
    ebc = np.zeros((P, 2, P), np.float32)
    for g in range(4):
        for s in range(9):
            sel[32 * g + s, s] = 1.0
        ebc[32 * g, 0, :] = 1.0
        for s in range(NSEQ):
            ebc[32 * g + 1 + s, 1, LS * s:LS * (s + 1)] = 1.0
    ebc[9, :, :] = 1.0
    return cos, np.ascontiguousarray(sin), ident, sel, ebc


def kernel(x_prompt, x_sample, cache_k, cache_v, state_pool, c_prompt, c_sample, w_ada, b_ada, w_in, attn_sinks, w_pool,
           pool_scale, w_out, ln_g, ln_b):
    import concourse.bacc as bacc
    from concourse.bass_utils import run_bass_kernel_spmd

    A = np.asarray
    cos, sin, ident, sel, ebc = tables()
    perm = head_dims()
    c_all = np.concatenate([A(c_prompt), A(c_sample)], 0)
    sinks = A(attn_sinks)[0]
    kc = A(cache_k)[0][..., perm].reshape(NSEQ, WIN, P)
    vcn = A(cache_v)[0].reshape(NSEQ, WIN, P)
    pair = np.concatenate([np.r_[HD * j:HD * (j + 1), HD * (4 + j):HD * (5 + j)] for j in range(4)])
    arrays = {
        "x_all": np.concatenate([A(x_prompt)[0], A(x_sample).reshape(-1, D)], 0).reshape(TILES, P, D),
        "cT_d": c_all.T.reshape(KT, P, 9).transpose(1, 0, 2),
        "bT_d": A(b_ada)[0].reshape(24, P).T,
        "w_ada": A(w_ada)[0].reshape(KT, P, 6, 512).transpose(2, 1, 0, 3),
        "w_in": A(w_in)[0][:, projection_columns()].reshape(KT, P, NBLK, P).transpose(2, 1, 0, 3),
        "w_out": A(w_out)[0][np.r_[pair, 512:1024]].reshape(KT, P, D),
        "w_pool": A(w_pool)[0].transpose(1, 0, 2),
        "pscale_d": A(pool_scale)[0].reshape(4, P).T,
        "sinkp_d": np.repeat(sinks.reshape(4, 2).T, QB, axis=0),
        "sinks_d": np.tile(np.repeat(sinks.reshape(2, 4).T, LS, axis=0), (2, 1)),
        "kcT": kc.transpose(0, 2, 1),
        "vc": vcn,
        "kc_tail": kc[:, LS:, :],
        "vc_tail": vcn[:, LS:, :],
        "histT": A(state_pool)[0].reshape(NSEQ, HIST, 4, P).transpose(2, 3, 0, 1),
        "ln_g": A(ln_g).reshape(1, D),
        "ln_b": A(ln_b).reshape(1, D),
        "ident_d": ident, "sel_d": sel, "ebc_d": ebc,
        "brow_d": A(b_ada)[0][2 * D:].reshape(1, 2, 512),
        "cos_d": cos, "sin_d": sin,
    }
    outs = {
        "y_out": (TILES, P, D), "kT_out": (P, 2 * WIN), "vT_out": (P, 2 * WIN), "upT_out": (4, P, HIST),
        "usT_out": (4, P, NSEQ, HIST), "kcT_out": (NSEQ, WIN - LS, P), "vc_out": (NSEQ, WIN - LS, P),
    }
    nc = bacc.Bacc("TRN2", target_bir_lowering=False, num_devices=1, dynamic_dma_scratch_size=1024)
    arrays = {n: np.ascontiguousarray(a) for n, a in arrays.items()}
    args = {n: nc.dram_tensor(n, a.shape, mybir.dt.from_np(a.dtype), kind="ExternalInput").ap() for n, a in arrays.items()}
    args.update({n: nc.dram_tensor(n, s, F32, kind="ExternalOutput").ap() for n, s in outs.items()})
    hybrid_step(nc, **args)
    r = run_bass_kernel_spmd(nc, [arrays], core_ids=[0]).results[0]

    inv = np.argsort(perm)
    y = r["y_out"].reshape(TOK, D)
    kn = r["kT_out"].T.reshape(2 * WIN, 2, HD)[..., inv]
    vn = r["vT_out"].T.reshape(2 * WIN, 2, HD)

    def sample_cache(old, new):
        return np.concatenate([old.reshape(NSEQ, WIN - LS, 2, HD), new[WIN:].reshape(NSEQ, LS, 2, HD)], 1)[None]

    up = r["upT_out"].transpose(2, 0, 1).reshape(1, 1, HIST, 512)
    us = r["usT_out"].transpose(2, 3, 0, 1).reshape(1, NSEQ, HIST, 512)
    return (y[:SEQ].reshape(1, SEQ, D), y[SEQ:].reshape(NSEQ, LS, D), kn[None, None, :WIN], vn[None, None, :WIN], up,
            sample_cache(r["kcT_out"].reshape(NSEQ, WIN - LS, 2, HD)[..., inv], kn), sample_cache(r["vc_out"], vn), us)
```

```python
import concourse.bass as bass
from concourse import mybir
import numpy as np

F32 = mybir.dt.float32
F32R = mybir.dt.float32r
ALU = mybir.AluOpType
ACT = mybir.ActivationFunctionType
AX = mybir.AxisListType

P = 128
D = 1024
SEQ = 1024
NSEQ = 8
LS = 16
TOK = SEQ + NSEQ * LS
KT = D // P
TILES = TOK // P
NCH = 3
CW = TOK // NCH
PW2 = SEQ - 2 * CW
HD = 64
QB = 64
NQ = 16
WIN = 128
HIST = 15
NSP = NSEQ // 2
NSTEP = NQ + NSP
ALPHA = float(2.0 ** 0.25)
EPS = 1e-5
SCALE = HD ** -0.5
UE = HIST + SEQ
UW = UE + NSEQ * (HIST + LS)
UB = (UW + 7) // 8 * 8

ADA = [0, 2, 1, 3, 4, 5]

K_BLK, V_BLK = 0, 1
GA_BLK = [2, 3, 4, 5]
Q_BLK = [6, 7, 8, 9]
GROUPS = [3, 2, 1, 0]
U_BLK = [10 + 2 * GROUPS.index(g) for g in range(4)]
GP_BLK = [11 + 2 * GROUPS.index(g) for g in range(4)]
NBLK = 18
RAW = 4
XS = 6


def unit_list():
    units = []
    for c in range(NCH):
        units += [("k", 0, c), ("v", 0, c)]
    units += [("ga", j, c) for j in range(4) for c in range(NCH)]
    units += [("q", j, c) for j in range(4) for c in range(NCH)]
    for s, g in enumerate(GROUPS):
        for c in range(NCH):
            units.append(("u", g, c))
            if s and c == 0:
                units.append(("z", GROUPS[s - 1], 0))
            if s and c == 1:
                units += [("z", GROUPS[s - 1], 1), ("z", GROUPS[s - 1], 2)]
        units += [("gp", g, c) for c in range(NCH - 1)]
        if s == 3:
            units += [("r", row, half) for row in range(2) for half in range(2)]
            units.append(("z", g, 0))
        units.append(("gp", g, NCH - 1))
    units += [("z", GROUPS[3], c) for c in range(1, NCH)]
    return units


UNITS = unit_list()
NU = len(UNITS)
BLOCK_OF = {"k": [K_BLK], "v": [V_BLK], "ga": GA_BLK, "q": Q_BLK, "u": U_BLK, "gp": GP_BLK}


def block_of(n):
    kind, j, _ = UNITS[n]
    return BLOCK_OF[kind][j] if kind in BLOCK_OF else None


LAST_UNIT = {block_of(n): n for n in range(NU) if block_of(n) is not None}
FIRST_UNIT = {block_of(n): n for n in reversed(range(NU)) if block_of(n) is not None}
LAST_PROJ = max(LAST_UNIT.values())
FREED_BY_ACT = ("v", "u", "r")


def freed_count(n):
    act = UNITS[n][0] in FREED_BY_ACT
    return act, sum((UNITS[m][0] in FREED_BY_ACT) == act for m in range(n + 1))


def count(kinds, n):
    return sum(UNITS[m][0] in kinds for m in range(n + 1))


def unit_index(kind, j, c):
    return UNITS.index((kind, j, c))


GATES = [n for n in range(NU) if UNITS[n][0] in ("ga", "gp")]

PLACES = [n for n in range(28, LAST_PROJ) if block_of(n) is not None] + [NU - 1] + [NU + m for m in range(1, 2 * TILES)]
SLOTS = {PLACES[4 * s // 3]: [s] for s in range(NSTEP + 2)}

H_ORDER = [(c, g) for pair in ((0, 1), (2, 3)) for c in range(2) for g in pair] + [(2, g) for g in range(4)]
POOL_LOW = [(0, 0), (0, 2), (1, 2), (2, 0), (2, 2)]
EARLY = 3


def low_count(c, g):
    return sum((x in POOL_LOW) == ((c, g) in POOL_LOW) for x in H_ORDER[:H_ORDER.index((c, g)) + 1])


def keys_of(i):
    if i >= NQ:
        return WIN, LS
    nk = min(i + 1, 3) * QB
    return min(nk, WIN), max(nk - WIN, 0)


def packed(i):
    return 3 <= i < NQ


OUTPUTS = [(t, 512 * half, 512) for t in range(TILES) for half in range(2)]
OUTPUTS[-1:] = [(TILES - 1, 512, 256), (TILES - 1, 768, 256)]

POOL_WO = (3, 4)


def wo_low_count(k):
    same = sum((x in POOL_WO) == (k in POOL_WO) for x in range(k + 1))
    return NBLK + same if k in POOL_WO else same


def seconds(i):
    return sum(keys_of(s)[1] > 0 for s in range(i + 1))


def hybrid_step(nc, x_all, cT_d, bT_d, w_ada, w_in, w_out, w_pool, pscale_d, sinkp_d, sinks_d, kcT, vc, kc_tail, vc_tail,
                histT, ln_g, ln_b, ident_d, sel_d, ebc_d, brow_d, cos_d, sin_d,
                y_out, kT_out, vT_out, upT_out, usT_out, kcT_out, vc_out):
    top = [nc.sbuf_base + 31 & ~31]

    def place(name, shape, dt=F32, at=None):
        size = 4
        for s in shape[1:]:
            size *= s
        if at is None:
            at = top[0]
            top[0] = (at + size + 31) & ~31
        return nc.alloc_sbuf_tensor_at(name, shape, dt, offset=at)

    def region(size):
        at = top[0]
        top[0] = (at + size + 31) & ~31
        return at

    r_h = region(2 * KT * TOK * 4)
    h_hi = place("h_hi", [P, KT, TOK], F32R, at=r_h)
    h_lo = place("h_lo", [P, KT, TOK], F32R, at=r_h + KT * TOK * 4)
    wo_hi = place("wo_hi", [P, KT, D], F32R, at=r_h)
    wo_lo = place("wo_lo", [P, KT, D], F32R, at=r_h + KT * TOK * 4)
    r_mx = region(KT * TOK * 4)
    xnT = place("xnT", [P, KT, TOK], at=r_mx)
    mixed = place("mixed", [P, KT, TOK], at=r_mx)
    r_q = region(4 * TOK * 4)
    qP = place("qP", [P, NQ, 4, QB], at=r_q)
    qS = place("qS", [P, NSEQ, 4, LS], at=r_q + NQ * 4 * QB * 4)
    xs = place("xs", [P, XS, D], at=r_q)
    wada_late = place("wada_late", [P, KT, 512], at=r_q)
    wada = [place(f"wada{i}", [P, KT, 512], at=r_h + o * TOK * 4) for i, o in enumerate((0, KT, KT // 2, KT + KT // 2))]
    r_a = top[0]
    Vc = place("Vc", [P, NQ, P])
    r_p = top[0]
    assert r_q + XS * D * 4 <= r_p
    Pb = place("Pb", [P, 2, 4, 192])
    PT1 = place("PT1", [P, 512])
    PT2 = place("PT2", [P, 512])
    vT = place("vT", [P, TOK], at=r_p)
    r_k = top[0]
    kT = place("kT", [P, TOK])
    th = place("th", [P, 2, CW])
    Ks = place("Ks", [P, NSP, 2, WIN])
    Vs = place("Vs", [P, NSP, 2, P])
    r_u = region(3 * UB * 4)
    rt1 = place("rt1", [P, 2, CW], at=r_u)
    rt2 = place("rt2", [P, 2, CW], at=r_u + 2 * CW * 4)
    cosT = place("cosT", [P, TOK], at=r_u + 4 * CW * 4)
    sinT = place("sinT", [P, TOK], at=r_u + 4 * CW * 4 + TOK * 4)
    assert 4 * CW * 4 + 2 * TOK * 4 <= 3 * UB * 4
    uext = place("uext", [P, UW], at=r_u)
    sA = place("sA", [P, UW], at=r_u + UB * 4)
    sB = place("sB", [P, UW], at=r_u + 2 * UB * 4)
    gateB = place("gateB", [P, 2, D], at=r_u)
    w_raw = place("w_raw", [P, RAW, KT, P])
    r_raw = top[0] - RAW * D * 4
    wo_raw = place("wo_raw", [P, RAW, D], at=r_raw)
    wo_rest = place("wo_rest", [P, KT - RAW, D], at=r_q)
    assert (KT - RAW) * D <= NQ * 4 * QB
    xf = place("xf", [P, 2, D], at=r_raw)
    yr = place("yr", [P, 2, D], at=r_raw + 2 * D * 4)
    lnG = place("lnG", [P, D], at=r_h + KT * D * 4)
    lnB = place("lnB", [P, D], at=r_h + (KT * TOK + KT * D) * 4)
    assert KT * (TOK - D) >= D
    r_hl = region(4 * KT * P * 4)
    w_hi = place("w_hi", [P, 2, KT, P], F32R, at=r_hl)
    w_lo = place("w_lo", [P, 2, KT, P], F32R, at=r_hl + 2 * KT * P * 4)
    m_hi = place("m_hi", [P, 2, KT, P], F32R, at=r_hl)
    m_lo = place("m_lo", [P, 2, KT, P], F32R, at=r_hl + 2 * KT * P * 4)
    part = place("part", [P, 2, 512])
    wp = place("wp", [P, 4, P])
    vnew = place("vnew", [LS, NSEQ, P])
    ident = place("ident", [P, P])
    sel = place("sel", [P, 9])
    ebc = place("ebc", [P, 2, P])
    cT = place("cT", [P, KT, 9])
    thc = place("thc", [P, KT, 9])
    cpad = place("cpad", [P, KT, 32])
    bT = place("bT", [P, 24])
    shT = place("shT", [P, KT, 9])
    s1T = place("s1T", [P, KT, 9])
    psc = place("psc", [P, 4])
    psc2 = place("psc2", [P, 4])
    nsp = place("nsp", [P, 4])
    nss = place("nss", [P, 2])
    skp = place("skp", [P, 4])
    sks = place("sks", [P, 2])
    bnst = place("bnst", [P, 2, 24])
    mv = place("mv", [P, 2, 2])
    veps = place("veps", [P, 2 * TILES])
    nmu = place("nmu", [P, 2 * TILES])
    rstd = place("rstd", [P, 2 * TILES])
    nmr = place("nmr", [P, 2 * TILES])
    mhalf = place("mhalf", [P, 1])
    mxs = place("mxs", [P, 2, 4])
    negm = place("negm", [P, 2, 4])
    sdl = place("sdl", [P, 2, 4])
    es = place("es", [P, 2, 4])
    rs = place("rs", [P, 2, 4])
    den = place("den", [P, 2, 4])
    rden = place("rden", [P, 2, 4])
    invc = place("invc", [P, HIST])
    fix = place("fix", [P, HIST])

    proj_ps = nc.alloc_psum_tensor("proj_ps", [P, 3, 512], F32)
    s_ps = nc.alloc_psum_tensor("s_ps", [P, 2, 512], F32)
    t_ps = nc.alloc_psum_tensor("t_ps", [P, 2, 512], F32)
    o_ps = nc.alloc_psum_tensor("o_ps", [P, 512], F32)

    sem = nc.alloc_semaphore
    ld_c = sem("ld_c"); ld_id = sem("ld_id"); ld_small = sem("ld_small"); ld_cs = sem("ld_cs"); ld_brow = sem("ld_brow")
    ld_ada = [[sem(f"ld_ada{i}_{h}") for h in range(2)] for i in range(4)]
    ld_late = sem("ld_late")
    ld_x = [sem(f"ld_x{i}") for i in range(XS)]
    ld_w = [sem(f"ld_w{i}") for i in range(RAW)]
    ld_wo = [sem(f"ld_wo{k}") for k in range(KT)]
    ld_kv = [sem(f"ld_kv{i}") for i in range(NSP)]
    ld_hist = sem("ld_hist"); ld_ln = sem("ld_ln")
    ld_xf = [sem(f"ld_xf{i}") for i in range(2)]
    st_y = [sem(f"st_y{i}") for i in range(2)]
    st_u = sem("st_u"); st_misc = sem("st_misc"); st_k = sem("st_k"); st_v = sem("st_v")
    ada_done = sem("ada_done"); sel_done = sem("sel_done"); xt_done = sem("xt_done"); unit_done = sem("unit_done")
    vt_done = sem("vt_done"); s_done = sem("s_done"); t_done = sem("t_done"); pv_done = sem("pv_done"); pv_low = sem("pv_low"); y_done = sem("y_done")
    thc_done = sem("thc_done"); xn_done = sem("xn_done"); ada_evac = sem("ada_evac"); xte_hi = sem("xte_hi")
    hhi_done = sem("hhi_done"); whi_done = sem("whi_done"); act_free = sem("act_free"); th_done = sem("th_done")
    exp_done = sem("exp_done"); es_done = sem("es_done"); pt1_done = sem("pt1_done"); mhi_done = sem("mhi_done")
    dve_step = sem("dve_step"); c_done = sem("c_done"); stats_done = sem("stats_done"); xte_lo = sem("xte_lo"); mod_done = sem("mod_done")
    hx_done = sem("hx_done"); hlo_v = sem("hlo_v"); dve_free = sem("dve_free"); rope_done = sem("rope_done")
    d_done = sem("d_done"); max_done = sem("max_done"); p_done = sem("p_done"); pt2_done = sem("pt2_done"); mix_done = sem("mix_done")
    vte_done = sem("vte_done"); mlo_v = sem("mlo_v"); mlo_p = sem("mlo_p"); r_done = sem("r_done"); g_done = sem("g_done"); wlo_v = sem("wlo_v"); consts_v = sem("consts_v")
    pool_step = sem("pool_step"); rstd_done = sem("rstd_done"); wlo_done = sem("wlo_done"); hlo_p = sem("hlo_p"); sum_done = sem("sum_done")
    yb_done = sem("yb_done")

    def cols(c):
        return slice(CW * c, CW * (c + 1))

    def w_out_raw(k):
        return wo_raw[:, (NBLK + k) % RAW, :] if k < RAW else wo_rest[:, k - RAW, :]

    def unit_bank(n):
        return s_ps[:, 0, :] if n == EARLY else proj_ps[:, n % 3, :]

    block = nc.Block()
    with block as block:

        @block.sync
        def _(sp):
            sp.dma_start(cT[:], cT_d).then_inc(ld_c, 16)

            def load_ada(a):
                for h in range(2):
                    k = slice(KT // 2 * h, KT // 2 * (h + 1))
                    sp.dma_start(wada[a][:, k, :], w_ada[ADA[a]][:, k, :]).then_inc(ld_ada[a][h], 16)

            def load_x(t):
                if t >= XS:
                    sp.wait_ge(xt_done, 2 * (t - XS + 1))
                sp.dma_start(xs[:, t % XS, :], x_all[t]).then_inc(ld_x[t % XS], 16)

            def load_w(b):
                if b >= RAW:
                    sp.wait_ge(whi_done, b - RAW + 1)
                    sp.wait_ge(wlo_done, b - RAW + 1)
                sp.dma_start(w_raw[:, b % RAW], w_in[b]).then_inc(ld_w[b % RAW], 16)

            def load_w_out(k):
                if k < RAW:
                    sp.wait_ge(whi_done, NBLK + k - RAW + 1)
                    sp.wait_ge(wlo_done, NBLK + k - RAW + 1)
                elif k == RAW:
                    sp.wait_ge(s_done, NQ)
                sp.dma_start(w_out_raw(k), w_out[k]).then_inc(ld_wo[k], 16)

            def load_kv(p):
                pair = slice(2 * p, 2 * p + 2)
                sp.dma_start(Ks[:, p], kcT[pair].rearrange("s p t -> p s t")).then_inc(ld_kv[p], 16)
                sp.dma_start(Vs[:, p], vc[pair].rearrange("s p d -> p s d")).then_inc(ld_kv[p], 16)

            def samples_u():
                return uext[:, UE:UW].rearrange("p (s t) -> p s t", t=HIST + LS)

            def load_history(s):
                if s == 0:
                    sp.wait_ge(rope_done, 15)
                else:
                    sp.wait_ge(d_done, s)
                    sp.wait_ge(st_u, 32 * s)
                sp.dma_start(samples_u()[:, :, 0:HIST], histT[GROUPS[s]]).then_inc(ld_hist, 16)

            def store_u(s):
                g = GROUPS[s]
                sp.wait_ge(act_free, freed_count(unit_index("u", g, NCH - 1))[1])
                sp.dma_start(upT_out[g], uext[:, UE - HIST:UE]).then_inc(st_u, 16)
                sp.dma_start(usT_out[g], samples_u()[:, :, LS:HIST + LS]).then_inc(st_u, 16)

            load_ada(0)
            load_x(0)
            sp.dma_start(ident[:], ident_d).then_inc(ld_id, 16)
            sp.dma_start(sel[:], sel_d).then_inc(ld_id, 16)
            sp.dma_start(bT[:], bT_d).then_inc(ld_id, 16)
            load_x(1)
            load_x(2)
            load_ada(1)
            load_w(0)
            load_w(1)
            load_x(3)
            load_x(4)
            load_x(5)
            load_x(6)
            load_x(7)
            load_x(8)
            load_ada(2)
            load_ada(3)
            sp.dma_start(cosT[:], cos_d).then_inc(ld_cs, 16)
            sp.dma_start(sinT[:], sin_d).then_inc(ld_cs, 16)
            load_w(2)
            sp.dma_start(ebc[:], ebc_d).then_inc(ld_small, 16)
            sp.dma_start(wp[:], w_pool).then_inc(ld_small, 16)
            sp.dma_start(psc[:], pscale_d).then_inc(ld_small, 16)
            sp.dma_start(skp[:], sinkp_d).then_inc(ld_small, 16)
            sp.dma_start(sks[:], sinks_d).then_inc(ld_small, 16)
            load_w(3)
            sp.wait_ge(xt_done, 2 * TILES)
            sp.dma_start(wada_late[:], w_ada[ADA[4]]).then_inc(ld_late, 16)
            load_w(4)
            sp.wait_ge(ada_done, 5)
            sp.dma_start(wada_late[:], w_ada[ADA[5]]).then_inc(ld_late, 16)
            load_w(5)
            sp.wait_ge(ada_evac, 6)
            sp.dma_start(part[9:10, :, :], brow_d).then_inc(ld_brow, 16)
            load_w(6)
            load_w(7)
            load_w(8)
            sp.wait_ge(rope_done, NCH)
            sp.dma_start(kT_out, kT[:, SEQ - WIN:TOK]).then_inc(st_k, 16)
            sp.wait_ge(act_free, NCH)
            sp.dma_start(vT_out, vT[:, SEQ - WIN:TOK]).then_inc(st_v, 16)
            sp.dma_start(kcT_out, kc_tail).then_inc(st_misc, 16)
            sp.dma_start(vc_out, vc_tail).then_inc(st_misc, 16)
            load_w(9)
            load_w(10)
            load_w(11)
            load_w(12)
            for p in range(NSP):
                load_kv(p)
            load_w(13)
            load_w(14)
            load_history(0)
            load_w(15)
            store_u(0)
            load_w(16)
            load_history(1)
            load_w(17)
            store_u(1)
            load_w_out(0)
            load_history(2)
            load_w_out(1)
            store_u(2)
            load_w_out(2)
            load_history(3)
            load_w_out(3)
            store_u(3)
            for k in range(RAW, KT):
                load_w_out(k)
            sp.wait_ge(unit_done, LAST_PROJ + 1)
            sp.dma_start(lnG[:], ln_g.to_broadcast([P, D])).then_inc(ld_ln, 16)
            sp.dma_start(lnB[:], ln_b.to_broadcast([P, D])).then_inc(ld_ln, 16)
            sp.wait_ge(whi_done, NBLK + KT)
            sp.wait_ge(wlo_v, KT - len(POOL_WO))
            sp.wait_ge(wlo_done, NBLK + len(POOL_WO))
            for t in range(TILES):
                if t >= 2:
                    sp.wait_ge(r_done, 2 * (t - 1))
                sp.dma_start(xf[:, t % 2, :], x_all[t]).then_inc(ld_xf[t % 2], 16)
                if t >= 1:
                    sp.wait_ge(yb_done, t)
                    sp.dma_start(y_out[t - 1], yr[:, (t - 1) % 2, :]).then_inc(st_y[(t - 1) % 2], 16)
            last = TILES - 1
            for half in range(2):
                w = slice(512 * half, 512 * (half + 1))
                sp.wait_ge(yb_done, TILES + half)
                sp.dma_start(y_out[last][:, w], yr[:, last % 2, w]).then_inc(st_y[last % 2], 16)
            sp.wait_ge(st_y[0], 16 * (TILES // 2 + 2))
            sp.wait_ge(st_y[1], 16 * (TILES // 2))
            sp.wait_ge(st_k, 16)
            sp.wait_ge(st_v, 16)
            sp.wait_ge(st_u, 32 * 4)
            sp.wait_ge(st_misc, 16 * 2)

        @block.tensor
        def _(pe):
            def ada(a, slices=range(KT)):
                if a < 4:
                    w = wada[a]
                else:
                    w = wada_late
                    pe.wait_ge(ld_late, 16 * (a - 3))
                if a == 0:
                    pe.wait_ge(c_done, 1)
                if a >= 2:
                    pe.wait_ge(ada_evac, a - 1)
                if a == 4:
                    pe.wait_ge(act_free, freed_count(EARLY)[1])
                for k in slices:
                    if a < 4 and k % (KT // 2) == 0:
                        pe.wait_ge(ld_ada[a][k // (KT // 2)], 16)
                    g = 32 * (k % 4)
                    mm = pe.matmul(s_ps[g:g + 32, a % 2, :], cpad[:, k, :], w[:, k, :], start=(k < 4), stop=(k >= 4), tile_position=(0, g))
                if slices[-1] == KT - 1:
                    mm.then_inc(ada_done, 1)

            def select(a):
                pe.wait_ge(ada_evac, a + 1)
                if a:
                    pe.wait_ge(mod_done, a)
                for m in range(4):
                    mm = pe.matmul(o_ps[:, 9 * m:9 * m + 9], part[:, a % 2, P * m:P * (m + 1)], sel[:], start=True, stop=True)
                mm.then_inc(sel_done, 1)

            def x_transpose(t):
                pe.wait_ge(xn_done, t + 1)
                if t == 0:
                    pe.wait_ge(ld_id, 48)
                for h in range(2):
                    if t:
                        pe.wait_ge(xte_hi if h else xte_lo, t)
                    for k in range(4):
                        mm = pe.transpose(t_ps[:, h, P * k:P * (k + 1)], xs[:, t % XS, P * (4 * h + k):P * (4 * h + k + 1)], ident[:])
                    mm.then_inc(xt_done, 1)

            def wait_bank(n):
                if n == EARLY:
                    pe.wait_ge(ada_evac, 3)
                elif n >= 3:
                    act, v = freed_count(n - 3 if n != EARLY + 3 else 0)
                    pe.wait_ge(act_free if act else dve_free, v)

            def unit(n, slices=range(KT)):
                kind, j, c = UNITS[n]
                bank = unit_bank(n)
                if slices[0] == 0:
                    wait_bank(n)
                if kind == "z":
                    pe.wait_ge(d_done, GROUPS.index(j) + 1)
                    pe.wait_ge(ld_small, 80)
                    dd = sB if j % 2 == 0 else sA
                    mm = pe.matmul(bank[:, 0:CW], wp[:, j, :], dd[:, cols(c)], start=True, stop=True)
                elif kind == "r":
                    pe.wait_ge(ld_brow, 16)
                    mm = pe.matmul(bank[:], ebc[:, j, :], part[:, c, :], start=True, stop=True)
                else:
                    b = block_of(n)
                    w = b % 2
                    if n == FIRST_UNIT[b] and slices[0] == 0:
                        pe.wait_ge(whi_done, b + 1)
                        pe.wait_ge(wlo_done, b + 1)
                    if kind == "k":
                        for k in slices:
                            if k % 2 == 0:
                                pe.wait_ge(hhi_done, H_ORDER.index((c, k // 2)) + 1)
                            pe.matmul(bank[:, 0:CW], w_hi[:, w, k, :], h_hi[:, k, cols(c)], start=(k == 0), stop=False)
                            pe.matmul(bank[:, 0:CW], w_lo[:, w, k, :], h_hi[:, k, cols(c)], start=False, stop=False)
                        for k in slices:
                            if k % 2 == 0:
                                pe.wait_ge(hlo_p if (c, k // 2) in POOL_LOW else hlo_v, low_count(c, k // 2))
                            mm = pe.matmul(bank[:, 0:CW], w_hi[:, w, k, :], h_lo[:, k, cols(c)], start=False, stop=(k == KT - 1))
                    else:
                        for k in slices:
                            hi, lo = h_hi[:, k, cols(c)], h_lo[:, k, cols(c)]
                            pe.matmul(bank[:, 0:CW], w_hi[:, w, k, :], hi, start=(k == 0), stop=False)
                            pe.matmul(bank[:, 0:CW], w_hi[:, w, k, :], lo, start=False, stop=False)
                            mm = pe.matmul(bank[:, 0:CW], w_lo[:, w, k, :], hi, start=False, stop=(k == KT - 1))
                if slices[-1] == KT - 1:
                    mm.then_inc(unit_done, 1)

            def v_transposes(m):
                pe.wait_ge(vte_done, m - 1) if m >= 2 else pe.wait_ge(xte_hi if m else xte_lo, TILES)
                if m == 0:
                    pe.wait_ge(act_free, NCH)
                for i in range(4):
                    if m < 4:
                        c = 4 * m + i
                        w = P if c < NQ - 1 else QB
                        mm = pe.transpose(t_ps[0:w, m % 2, P * i:P * (i + 1)], vT[:, QB * c:QB * c + w], ident[:])
                    else:
                        s = 4 * (m - 4) + i
                        mm = pe.transpose(t_ps[0:LS, m % 2, P * i:P * (i + 1)], vT[:, SEQ + LS * s:SEQ + LS * (s + 1)], ident[:])
                mm.then_inc(vt_done, 1)

            def scores(i):
                pe.wait_ge(rope_done, NCH + 3 * NCH + min(QB * i // CW, NCH - 1) + 1)
                if i == 0:
                    pe.wait_ge(ada_evac, 6)
                else:
                    pe.wait_ge(exp_done, i)
                for p in range(2 if i < NQ else 0):
                    for kv in range(2):
                        r = slice(HD * kv, HD * (kv + 1))
                        nk = sum(keys_of(i))
                        k0 = QB * (i + 1) - nk
                        mm = pe.matmul(s_ps[:, kv, 192 * p:192 * p + nk], qP[r, i, 2 * p:2 * p + 2, :],
                                       kT[r, k0:k0 + nk], start=True, stop=True, tile_position=(HD * kv, 0))
                for kv in range(0 if i < NQ else 2):
                    r = slice(HD * kv, HD * (kv + 1))
                    if i >= NQ:
                        sp_ = i - NQ
                        if kv == 0:
                            pe.wait_ge(ld_kv[sp_], 32)
                        for e in range(2):
                            t0 = SEQ + LS * (2 * sp_ + e)
                            q = qS[r, 2 * sp_ + e, :, :]
                            o = s_ps[HD * e:HD * (e + 1), kv, :]
                            pe.matmul(o[:, 0:WIN], q, Ks[r, sp_, e, :], start=True, stop=True, tile_position=(HD * kv, HD * e))
                            mm = pe.matmul(o[:, WIN:WIN + LS], q, kT[r, t0:t0 + LS], start=True, stop=True, tile_position=(HD * kv, HD * e))
                mm.then_inc(s_done, 1)

            def p_transposes(i):
                pe.wait_ge(p_done, i + 1)
                if i:
                    pe.wait_ge(pt1_done, i)
                    if seconds(i - 1):
                        pe.wait_ge(pt2_done, seconds(i - 1))
                else:
                    pe.wait_ge(vte_done, 6)
                k1, k2 = keys_of(i)
                if packed(i):
                    rows = Pb[:, i % 2].rearrange("p j n -> p (j n)")
                    for m in range(6):
                        mm = pe.transpose(t_ps[:, m // 4, P * (m % 4):P * (m % 4 + 1)], rows[:, P * m:P * (m + 1)], ident[:])
                    mm.then_inc(t_done, 1)
                    return
                for j in range(4 if i < NQ else 2):
                    mm = pe.transpose(t_ps[0:k1, 0, P * j:P * (j + 1)], Pb[:, i % 2, j, 0:k1], ident[:])
                    if k2:
                        mm = pe.transpose(t_ps[0:k2, 1, P * j:P * (j + 1)], Pb[:, i % 2, j, WIN:WIN + k2], ident[:])
                mm.then_inc(t_done, 1)

            def values(i):
                pe.wait_ge(pt1_done, i + 1)
                if seconds(i):
                    pe.wait_ge(pt2_done, seconds(i))
                if i:
                    pe.wait_ge(mix_done, i)
                k1, k2 = keys_of(i)
                if packed(i):
                    block = [(PT1 if m < 4 else PT2)[:, P * (m % 4):P * (m % 4 + 1)] for m in range(6)]
                    heads = [(slice(HD * kv, HD * (kv + 1)), HD * kv) for kv in range(2)]
                    for kv, (d, col) in enumerate(heads):
                        pe.matmul(o_ps[d, 0:P], Vc[:, i - 2, d], block[3 * kv], start=True, stop=False, tile_position=(0, col))
                        pe.matmul(o_ps[d, 0:P], Vc[0:QB, i, d], block[3 * kv + 1][0:QB], start=False, stop=True,
                                  tile_position=(0, col)).then_inc(pv_low, 1)
                    for kv, (d, col) in enumerate(heads):
                        pe.matmul(o_ps[d, P:2 * P], Vc[:, i - 1, d], block[3 * kv + 2], start=True, stop=False, tile_position=(0, col))
                    pe.wait_ge(pv_low, 2 * sum(packed(s) for s in range(i + 1)))
                    for kv, (d, col) in enumerate(heads):
                        mm = pe.matmul(o_ps[d, P:2 * P], Vc[QB:P, i - 3, d], block[3 * kv + 1][QB:P], start=False, stop=True,
                                       tile_position=(QB, col))
                    mm.then_inc(pv_done, 1)
                    return
                for kv in range(2):
                    d = slice(HD * kv, HD * (kv + 1))
                    if i < NQ:
                        o = o_ps[d, 0:256]
                        mm = pe.matmul(o, Vc[0:k1, max(i - 2, 0), d], PT1[0:k1, 256 * kv:256 * (kv + 1)], start=True, stop=not k2,
                                       tile_position=(0, HD * kv))
                        if k2:
                            mm = pe.matmul(o, Vc[0:QB, i, d], PT2[0:QB, 256 * kv:256 * (kv + 1)], start=False, stop=True,
                                           tile_position=(0, HD * kv))
                    else:
                        sp_ = i - NQ
                        for e in range(2):
                            o = o_ps[d, HD * e:HD * (e + 1)]
                            w = slice(P * kv + HD * e, P * kv + HD * (e + 1))
                            pe.matmul(o, Vs[:, sp_, e, d], PT1[:, w], start=True, stop=False, tile_position=(0, HD * kv))
                            mm = pe.matmul(o, vnew[0:LS, 2 * sp_ + e, d], PT2[0:LS, w], start=False, stop=True, tile_position=(0, HD * kv))
                mm.then_inc(pv_done, 1)

            def slot(i):
                if 0 <= i - 2 < NSTEP:
                    values(i - 2)
                if 0 <= i - 1 < NSTEP:
                    p_transposes(i - 1)
                if i < NSTEP:
                    scores(i)

            def output(ms, k):
                for m in ms:
                    t, w0, n = OUTPUTS[m]
                    o = proj_ps[:, (NU + m) % 3, 0:n]
                    w = slice(w0, w0 + n)
                    pe.matmul(o, m_hi[:, t % 2, k, :], wo_hi[:, k, w], start=(k == 0), stop=False)
                    pe.matmul(o, m_hi[:, t % 2, k, :], wo_lo[:, k, w], start=False, stop=False)
                    mm = pe.matmul(o, m_lo[:, t % 2, k, :], wo_hi[:, k, w], start=False, stop=(k == KT - 1))
                    if k == KT - 1:
                        mm.then_inc(y_done, 1)

            low, high = range(KT // 2), range(KT // 2, KT)
            ada(0)
            x_transpose(0)
            x_transpose(1)
            ada(1, low)
            x_transpose(2)
            ada(1, high)
            select(0)
            select(1)
            unit(0, low)
            x_transpose(3)
            unit(1, low)
            x_transpose(4)
            x_transpose(5)
            ada(2)
            x_transpose(6)
            select(2)
            ada(3, low)
            unit(2, low)
            ada(3, high)
            x_transpose(7)
            select(3)
            x_transpose(8)
            unit(3, low)
            for n in range(4):
                unit(n, high)
            after = {6: [(v_transposes, 0), (v_transposes, 1)], 7: [(ada, 4), (v_transposes, 2), (v_transposes, 3)],
                     8: [(v_transposes, 4), (v_transposes, 5)], 11: [(ada, 5)]}
            for n in range(4, NU):
                unit(n)
                for f, a in after.get(n, []):
                    f(a)
                for i in SLOTS.get(n, []):
                    slot(i)
            pe.wait_ge(mhi_done, 1)
            pe.wait_ge(mlo_v, 1)
            wait_bank(NU)
            wait_bank(NU + 1)
            for k in range(KT):
                pe.wait_ge(whi_done, NBLK + k + 1)
                pe.wait_ge(wlo_done if k in POOL_WO else wlo_v, wo_low_count(k))
                output((0, 1), k)
            for i in SLOTS.get(NU + 1, []):
                slot(i)
            for m in range(2, len(OUTPUTS)):
                t = OUTPUTS[m][0]
                if OUTPUTS[m][1] == 0:
                    pe.wait_ge(mhi_done, t + 1)
                    pe.wait_ge(mlo_p, t)
                if m < 3:
                    wait_bank(NU + m)
                else:
                    pe.wait_ge(g_done, m - 2)
                for k in range(KT):
                    output((m,), k)
                for i in SLOTS.get(NU + m, []):
                    slot(i)

        @block.scalar
        def _(act):
            def normalise(t):
                act.wait_ge(rstd_done, t + 1)
                act.activation(xs[:, t % XS, :], xs[:, t % XS, :], ACT.Identity, bias=nmr[:, t:t + 1], scale=rstd[:, t:t + 1]).then_inc(xn_done, 1)

            def evac_ada(a):
                act.wait_ge(ada_done, a + 1)
                if a >= 2:
                    act.wait_ge(sel_done, min(a - 1, 4))
                act.activation(part[:, a % 2, :], s_ps[:, a % 2, :], ACT.Identity, scale=0.5).then_inc(ada_evac, 1)

            def evac_xt(t):
                if 3 <= t < 6:
                    act.wait_ge(xt_done, 2 * t + 1)
                    act.activation(xnT[:, 0:4, P * t:P * (t + 1)], t_ps[:, 0, :].rearrange("p (k t) -> p k t", t=P), ACT.Copy).then_inc(xte_lo, 1)
                act.wait_ge(xt_done, 2 * t + 2)
                act.activation(xnT[:, 4:8, P * t:P * (t + 1)], t_ps[:, 1, :].rearrange("p (k t) -> p k t", t=P), ACT.Copy).then_inc(xte_hi, 1)

            def h_high(c, groups=range(4)):
                for g in groups:
                    act.wait_ge(hx_done, H_ORDER.index((c, g)) + 1)
                    act.activation(h_hi[:, 2 * g:2 * g + 2, cols(c)], xnT[:, 2 * g:2 * g + 2, cols(c)], ACT.Copy).then_inc(hhi_done, 1)

            def w_high(b):
                act.wait_ge(ld_w[b % RAW], 16 * (b // RAW + 1))
                if b >= 2:
                    act.wait_ge(unit_done, LAST_UNIT[b - 2] + 1)
                act.activation(w_hi[:, b % 2], w_raw[:, b % RAW], ACT.Copy).then_inc(whi_done, 1)

            def evac_unit(n):
                kind, j, c = UNITS[n]
                src = unit_bank(n)[:, 0:CW]
                if kind in ("k", "q", "z"):
                    return
                act.wait_ge(unit_done, n + 1)
                if kind == "v":
                    act.activation(vT[:, cols(c)], src, ACT.Copy).then_inc(act_free, 1)
                elif kind in ("ga", "gp"):
                    i = GATES.index(n)
                    if i >= 2:
                        act.wait_ge(dve_free, freed_count(GATES[i - 2])[1])
                    act.activation(th[:, i % 2, :], src, ACT.Tanh, scale=0.5).then_inc(th_done, 1)
                elif kind == "u":
                    if c == 0:
                        s = GROUPS.index(j)
                        if s == 0:
                            act.wait_ge(rope_done, 15)
                        else:
                            act.wait_ge(d_done, s)
                            act.wait_ge(st_u, 32 * s)
                    if c < 2:
                        act.activation(uext[:, HIST + CW * c:HIST + CW * (c + 1)], src, ACT.Copy).then_inc(act_free, 1)
                    else:
                        act.activation(uext[:, HIST + 2 * CW:UE], src[:, 0:PW2], ACT.Copy)
                        act.activation(uext[:, UE:UW].rearrange("p (s t) -> p s t", t=HIST + LS)[:, :, HIST:],
                                       src[:, PW2:CW].rearrange("p (s t) -> p s t", t=LS), ACT.Copy).then_inc(act_free, 1)
                else:
                    if j == 0 and c == 0:
                        act.wait_ge(d_done, 4)
                        act.wait_ge(st_u, 32 * 4)
                    act.activation(gateB[:, j, 512 * c:512 * (c + 1)], proj_ps[:, n % 3, :], ACT.Copy).then_inc(act_free, 1)

            def slot(i):
                if 0 <= i - 1 < NSTEP:
                    k1, _ = keys_of(i - 1)
                    w = 512 if i - 1 < NQ else 256
                    act.wait_ge(t_done, i)
                    if i >= 2:
                        act.wait_ge(pv_done, i - 1)
                    act.activation(PT1[0:k1, 0:w], t_ps[0:k1, 0, 0:w], ACT.Copy).then_inc(pt1_done, 1)
                if i < NSTEP:
                    act.wait_ge(max_done, i + 1)
                    if i == 0:
                        act.wait_ge(st_v, 16)
                    if i >= 2:
                        act.wait_ge(t_done, i - 1)
                        act.wait_ge(p_done, i - 1)
                    nj, nk = (4 if i < NQ else 2), sum(keys_of(i))
                    act.activation(es[:, i % 2, 0:nj], sdl[:, i % 2, 0:nj], ACT.Exp).then_inc(es_done, 1)
                    for j in range(nj):
                        src = s_ps[:, j // 2, 192 * (j % 2):192 * (j % 2) + nk] if i < NQ else s_ps[:, j, 0:nk]
                        e = act.activation(Pb[:, i % 2, j, 0:nk], src, ACT.Exp, bias=negm[:, i % 2, j:j + 1], scale=SCALE,
                                           accum_out=rs[:, i % 2, j:j + 1])
                    e.then_inc(exp_done, 1)

            def wo_high(k):
                act.wait_ge(ld_wo[k], 16)
                act.activation(wo_hi[:, k, :], w_out_raw(k), ACT.Copy).then_inc(whi_done, 1)

            def mixed_high(t):
                act.wait_ge(mix_done, 2 * t + 2 if t < TILES - 1 else NSTEP)
                act.wait_ge(dve_free, freed_count(unit_index("z", GROUPS[3], t // 3))[1])
                if t >= 2:
                    act.wait_ge(y_done, 2 * (t - 1))
                act.activation(m_hi[:, t % 2], mixed[:, :, P * t:P * (t + 1)], ACT.Copy).then_inc(mhi_done, 1)

            act.wait_ge(ld_c, 16)
            act.activation(thc[:], cT[:], ACT.Tanh, scale=0.5).then_inc(thc_done, 1)
            normalise(0)
            evac_ada(0)
            normalise(1)
            evac_xt(0)
            normalise(2)
            evac_xt(1)
            evac_xt(2)
            w_high(0)
            w_high(1)
            evac_ada(1)
            h_high(0, (0, 1))
            normalise(3)
            normalise(4)
            evac_xt(3)
            normalise(5)
            evac_xt(4)
            normalise(6)
            evac_xt(5)
            evac_ada(2)
            normalise(7)
            h_high(1, (0, 1))
            evac_xt(6)
            normalise(8)
            evac_ada(3)
            evac_xt(7)
            evac_xt(8)
            h_high(0, (2, 3))
            h_high(1, (2, 3))
            evac_unit(1)
            h_high(2)
            evac_unit(3)
            w_high(2)
            evac_unit(5)
            w_high(3)
            after = {7: 4, 11: 5}
            for n in range(6, NU):
                b = block_of(n)
                evac_unit(n)
                if n in after:
                    evac_ada(after[n])
                if n == NU - 1:
                    for k in range(1, 6):
                        wo_high(k)
                for i in SLOTS.get(n, []):
                    slot(i)
                if b is not None and LAST_UNIT[b] == n and b + 2 < NBLK:
                    w_high(b + 2)
                if UNITS[n] == ("z", GROUPS[3], 0):
                    mixed_high(0)
                if n == LAST_PROJ:
                    wo_high(0)
            for k in range(6, KT):
                wo_high(k)
            mixed_high(1)
            for m in range(2 * TILES):
                if m % 2 == 0 and 2 <= m // 2 + 1 < TILES:
                    mixed_high(m // 2 + 1)
                for i in SLOTS.get(NU + m, []):
                    slot(i)

        @block.vector
        def _(dve):
            steps = [0]

            def link(ins):
                steps[0] += 1
                ins.then_inc(dve_step, 1)
                dve.wait_ge(dve_step, steps[0])

            def stats(t, src):
                b = t % 2
                dve.bn_stats(bnst[:, b, 0:6], src[:, 0:512])
                link(dve.bn_stats(bnst[:, b, 6:12], src[:, 512:1024]))
                mean_var(t)

            def mean_var(t, pieces=2):
                b = t % 2
                link(dve.bn_aggr(mv[:, b, :], bnst[:, b, 0:6 * pieces]))
                dve.tensor_scalar(nmu[:, t:t + 1], mv[:, b, 0:1], -1.0, None, ALU.mult)
                dve.tensor_scalar(veps[:, t:t + 1], mv[:, b, 1:2], EPS, None, ALU.add).then_inc(stats_done, 1)

            def x_stats(t):
                dve.wait_ge(ld_x[t % XS], 16 * (t // XS + 1))
                stats(t, xs[:, t % XS, :])

            def w_low(b):
                dve.wait_ge(whi_done, b + 1)
                dve.tensor_tensor(w_lo[:, b % 2], w_raw[:, b % RAW], w_hi[:, b % 2].bitcast(F32), ALU.subtract).then_inc(wlo_done, 1)

            def evac_xt(t):
                dve.wait_ge(xt_done, 2 * t + 1)
                dve.tensor_copy(xnT[:, 0:4, P * t:P * (t + 1)], t_ps[:, 0, :].rearrange("p (k t) -> p k t", t=P)).then_inc(xte_lo, 1)

            def modulation(a):
                dve.wait_ge(sel_done, a + 1)
                if a == 0:
                    dve.wait_ge(ld_id, 48)
                ci = ADA[a]
                dst = shT if ci < 2 else s1T
                k0 = 4 * (ci % 2)
                dve.scalar_tensor_tensor(dst[:, k0:k0 + 4, :], o_ps[:, 0:36].rearrange("p (k s) -> p k s", s=9), 0.0 if ci < 2 else 1.0,
                                         bT[:, 4 * ci:4 * ci + 4].unsqueeze(2).to_broadcast([P, 4, 9]), ALU.add, ALU.add).then_inc(mod_done, 1)

            def h_ops(c, groups=range(4)):
                dve.wait_ge(mod_done, groups[-1] + 1)
                tiles = 3 * c + 3 if c < 2 else TILES - 1
                dve.wait_ge(xte_hi, tiles)
                dve.wait_ge(xte_lo, tiles)
                pw = CW if c < 2 else PW2
                for g in groups:
                    for k in (2 * g, 2 * g + 1):
                        x = xnT[:, k, CW * c:CW * c + pw]
                        last = dve.tensor_scalar(x, x, s1T[:, k, 0:1], shT[:, k, 0:1], ALU.mult, ALU.add)
                    if c < 2:
                        last.then_inc(hx_done, 1)
                if c == 2:
                    link(last)

            def h_samples(half):
                dve.wait_ge(xte_hi, TILES)
                dve.wait_ge(xte_lo, TILES)
                ks = slice(KT // 2 * half, KT // 2 * (half + 1))
                v = xnT[:, ks, SEQ:TOK].rearrange("p k (s t) -> p k s t", t=LS)
                link(dve.tensor_tensor(v, v, s1T[:, ks, 1:9].unsqueeze(3).to_broadcast([P, KT // 2, NSEQ, LS]), ALU.mult))
                dve.tensor_tensor(v, v, shT[:, ks, 1:9].unsqueeze(3).to_broadcast([P, KT // 2, NSEQ, LS]), ALU.add).then_inc(hx_done, 2)

            def h_low(c, groups):
                for g in groups:
                    dve.wait_ge(hhi_done, H_ORDER.index((c, g)) + 1)
                    w = slice(2 * g, 2 * g + 2)
                    dve.tensor_tensor(h_lo[:, w, cols(c)], xnT[:, w, cols(c)], h_hi[:, w, cols(c)].bitcast(F32), ALU.subtract).then_inc(hlo_v, 1)

            def evac_unit(n):
                kind, j, c = UNITS[n]
                src = unit_bank(n)[:, 0:CW]
                if kind in ("v", "u", "r"):
                    return
                if kind in ("k", "q"):
                    i = count(("k", "q"), n) - 1
                    if i == 0:
                        dve.wait_ge(ld_cs, 32)
                    if kind == "q" and j == 0 and c == 0:
                        dve.wait_ge(ada_done, 6)
                    dve.wait_ge(unit_done, n + 1)
                    r = i % 2
                    dve.stream_shuffle(rt1[:, r, :], src, [(m + 16) % 32 for m in range(32)])
                    dve.tensor_tensor(rt2[:, r, :], src, cosT[:, cols(c)], ALU.mult).then_inc(dve_free, 1)
                    dve.wait_ge(dve_free, freed_count(n)[1])
                    link(dve.tensor_tensor(rt1[:, r, :], rt1[:, r, :], sinT[:, cols(c)], ALU.mult))
                    if kind == "k":
                        dve.tensor_tensor(kT[:, cols(c)], rt1[:, r, :], rt2[:, r, :], ALU.add).then_inc(rope_done, 1)
                        return
                    pw = CW if c < 2 else PW2
                    nq = CW // QB
                    a, b = (x[:, r, 0:pw].rearrange("p (q t) -> p q t", t=QB) for x in (rt1, rt2))
                    last = dve.tensor_tensor(qP[:, nq * c:nq * c + pw // QB, j, :], a, b, ALU.add)
                    if c == 2:
                        a, b = (x[:, r, pw:CW].rearrange("p (s t) -> p s t", t=LS) for x in (rt1, rt2))
                        last = dve.tensor_tensor(qS[:, :, j, :], a, b, ALU.add)
                    last.then_inc(rope_done, 1)
                elif kind in ("ga", "gp"):
                    i = count(("ga", "gp"), n) - 1
                    dve.wait_ge(th_done, i + 1)
                    if n == FIRST_UNIT[GA_BLK[0]]:
                        dve.wait_ge(hlo_p, len(POOL_LOW))
                        dve.wait_ge(hhi_done, 12)
                    dst = mixed[:, j if kind == "ga" else 4 + j, cols(c)]
                    dve.scalar_tensor_tensor(dst, th[:, i % 2, :], 1.0, src, ALU.add, ALU.mult).then_inc(dve_free, 1)
                else:
                    dve.wait_ge(unit_done, n + 1)
                    dve.wait_ge(dve_free, freed_count(unit_index("gp", j, c))[1])
                    dst = mixed[:, 4 + j, cols(c)]
                    dve.scalar_tensor_tensor(dst, src, psc2[:, j:j + 1], dst, ALU.mult, ALU.mult).then_inc(dve_free, 1)

            def pool_mean(g):
                w = 2 << g
                s, d = (sA, sB) if g % 2 == 0 else (sB, sA)
                dve.wait_ge(sum_done, GROUPS.index(g) + 1)
                link(dve.tensor_tensor(fix[:, 0:w - 1], s[:, HIST:HIST + w - 1], invc[:, 0:w - 1], ALU.mult))
                dve.scalar_tensor_tensor(d[:, w - 1:SEQ], s[:, HIST + w - 1:UE], 1.0 / w, uext[:, HIST + w - 1:UE], ALU.mult, ALU.subtract)
                dve.tensor_tensor(d[:, 0:w - 1], fix[:, 0:w - 1], uext[:, HIST:HIST + w - 1], ALU.subtract)

                def samples(x):
                    return x[:, UE:UW].rearrange("p (s t) -> p s t", t=HIST + LS)[:, :, HIST:]

                dve.scalar_tensor_tensor(d[:, SEQ:TOK].rearrange("p (s t) -> p s t", t=LS), samples(s), 1.0 / w, samples(uext),
                                         ALU.mult, ALU.subtract).then_inc(d_done, 1)

            def evac_v(m):
                dve.wait_ge(vt_done, m + 1)
                if m < 4:
                    if m < 3:
                        dve.tensor_copy(Vc[:, 4 * m:4 * m + 4, :], t_ps[:, m % 2, :].rearrange("p (c d) -> p c d", d=P)).then_inc(vte_done, 1)
                    else:
                        dve.tensor_copy(Vc[:, 12:15, :], t_ps[:, 1, 0:3 * P].rearrange("p (c d) -> p c d", d=P))
                        dve.tensor_copy(Vc[0:QB, 15, :], t_ps[0:QB, 1, 3 * P:4 * P]).then_inc(vte_done, 1)
                else:
                    dve.tensor_copy(vnew[:, 4 * (m - 4):4 * (m - 3), :], t_ps[0:LS, m % 2, :].rearrange("p (c d) -> p c d", d=P)).then_inc(vte_done, 1)

            def mix(i):
                dve.wait_ge(pv_done, i + 1)
                if i < NQ:
                    g = mixed[:, 0:4, QB * i:QB * (i + 1)]
                    dve.scalar_tensor_tensor(g, o_ps[:, 0:256].rearrange("p (j t) -> p j t", t=QB), 0.5, g, ALU.mult, ALU.mult).then_inc(mix_done, 1)
                else:
                    for e in range(2):
                        t0 = SEQ + LS * (2 * (i - NQ) + e)
                        g = mixed[:, 0:4, t0:t0 + LS]
                        last = dve.scalar_tensor_tensor(g, o_ps[:, HD * e:HD * (e + 1)].rearrange("p (j t) -> p j t", t=LS), 0.5, g, ALU.mult, ALU.mult)
                    last.then_inc(mix_done, 1)

            def slot(i):
                if 0 <= i - 2 < NSTEP:
                    mix(i - 2)
                if 0 <= i - 1 < NSTEP and keys_of(i - 1)[1]:
                    k2 = keys_of(i - 1)[1]
                    w = 512 if i - 1 < NQ else 256
                    if packed(i - 1):
                        k2, w = P, 256
                    dve.wait_ge(t_done, i)
                    if i >= 2:
                        dve.wait_ge(pv_done, i - 1)
                    dve.tensor_copy(PT2[0:k2, 0:w], t_ps[0:k2, 1, 0:w]).then_inc(pt2_done, 1)
                if i < NSTEP:
                    b, nk = i % 2, sum(keys_of(i))
                    dve.wait_ge(s_done, i + 1)
                    if i < NQ:
                        nj, sink = 4, nsp
                        src = s_ps[:, :, 0:384].rearrange("p b (r n) -> p b r n", n=192)[:, :, :, 0:nk]
                        out = mxs[:, b, :].rearrange("p (b r) -> p b r", r=2)
                    else:
                        nj, sink = 2, nss
                        src, out = s_ps[:, :, 0:nk], mxs[:, b, 0:2]
                    link(dve.tensor_reduce(out, src, AX.X, ALU.max))
                    link(dve.scalar_tensor_tensor(negm[:, b, 0:nj], mxs[:, b, 0:nj], -SCALE, sink[:, 0:nj], ALU.mult, ALU.min))
                    dve.tensor_tensor(sdl[:, b, 0:nj], negm[:, b, 0:nj], sink[:, 0:nj], ALU.subtract).then_inc(max_done, 1)
                    dve.wait_ge(exp_done, i + 1)
                    dve.wait_ge(es_done, i + 1)
                    link(dve.tensor_tensor(den[:, b, 0:nj], rs[:, b, 0:nj], es[:, b, 0:nj], ALU.add))
                    link(dve.reciprocal(rden[:, b, 0:nj], den[:, b, 0:nj]))
                    p = Pb[:, b, 0:nj, 0:nk]
                    dve.tensor_tensor(p, p, rden[:, b, 0:nj].unsqueeze(2).to_broadcast([P, nj, nk]), ALU.mult).then_inc(p_done, 1)

            def wo_low(k):
                dve.wait_ge(whi_done, NBLK + k + 1)
                dve.tensor_tensor(wo_lo[:, k, :], w_out_raw(k), wo_hi[:, k, :].bitcast(F32), ALU.subtract).then_inc(wlo_v, 1)

            link(dve.memset(cpad[:], 0.0))
            dve.memset(mhalf[:], -0.5).then_inc(consts_v, 1)
            dve.wait_ge(thc_done, 1)
            dve.scalar_tensor_tensor(cpad[:, :, 0:9], thc[:], 1.0, cT[:], ALU.add, ALU.mult).then_inc(c_done, 1)
            for m in range(HIST):
                last = dve.memset(invc[:, m:m + 1], 1.0 / (m + 1))
            link(last)
            x_stats(0)
            x_stats(1)
            x_stats(2)
            evac_xt(0)
            evac_xt(1)
            evac_xt(2)
            w_low(0)
            modulation(0)
            w_low(1)
            modulation(1)
            h_ops(0, (0, 1))
            x_stats(3)
            h_low(0, (1,))
            x_stats(4)
            x_stats(5)
            x_stats(6)
            x_stats(7)
            x_stats(8)
            h_ops(1, (0, 1))
            modulation(2)
            h_low(1, (0, 1))
            evac_xt(6)
            evac_xt(7)
            modulation(3)
            h_ops(0, (2, 3))
            evac_xt(8)
            h_ops(1, (2, 3))
            h_low(0, (3,))
            h_ops(2, (0, 1))
            h_low(1, (3,))
            h_samples(0)
            h_ops(2, (2, 3))
            h_samples(1)
            evac_unit(0)
            h_low(2, (1, 3))
            evac_unit(2)
            evac_unit(4)
            after = {6: [0, 1], 7: [2, 3], 8: [4, 5]}
            for n in range(6, NU):
                if n == 9:
                    dve.wait_ge(ld_small, 16 * 5)
                    dve.tensor_scalar(psc2[:], psc[:], 0.5, None, ALU.mult)
                    dve.tensor_scalar(nsp[:], skp[:], -1.0, None, ALU.mult)
                    link(dve.tensor_scalar(nss[:], sks[:], -1.0, None, ALU.mult))
                kind, j, c = UNITS[n]
                evac_unit(n)
                if kind == "gp" and c == (NCH - 1 if j != GROUPS[3] else 0):
                    pool_mean(j)
                for m in after.get(n, []):
                    evac_v(m)
                if UNITS[n] == ("z", GROUPS[3], 0):
                    dve.wait_ge(mhi_done, 1)
                    dve.tensor_tensor(m_lo[:, 0], mixed[:, :, 0:P], m_hi[:, 0].bitcast(F32), ALU.subtract).then_inc(mlo_v, 1)
                if n >= LAST_PROJ:
                    wo_low(n - LAST_PROJ)
                for i in SLOTS.get(n, []):
                    slot(i)
            for k in range(5, KT):
                wo_low(k)
            for m, (t, w0, n) in enumerate(OUTPUTS):
                row = 0 if t < TILES - 1 else 1
                w = slice(w0, w0 + n)
                r = yr[:, t % 2, w]
                dve.wait_ge(y_done, m + 1)
                if m == 0:
                    dve.wait_ge(act_free, freed_count(unit_index("r", 1, 1))[1])
                    dve.wait_ge(whi_done, NBLK + KT)
                    dve.wait_ge(wlo_done, NBLK + len(POOL_WO))
                if t >= 2 and w0 == 0:
                    dve.wait_ge(st_y[t % 2], 16 * (t // 2))
                dve.tensor_tensor(r, proj_ps[:, (NU + m) % 3, 0:n], gateB[:, row, w], ALU.mult).then_inc(g_done, 1)
                dve.wait_ge(g_done, m + 1)
                dve.wait_ge(ld_xf[t % 2], 16 * (t // 2 + 1))
                dve.scalar_tensor_tensor(r, xf[:, t % 2, w], ALPHA, r, ALU.mult, ALU.add).then_inc(r_done, 1)
                dve.wait_ge(r_done, m + 1)
                size = 512 if t < TILES - 1 else 256
                for c in range(w0 // size, (w0 + n) // size):
                    last = dve.bn_stats(bnst[:, (TILES + t) % 2, 6 * c:6 * c + 6], yr[:, t % 2, size * c:size * (c + 1)])
                if w0 + n == D:
                    link(last)
                    mean_var(TILES + t, D // size)
                    dve.wait_ge(stats_done, TILES + t + 1)
                    if t == 0:
                        dve.wait_ge(ld_ln, 32)
                    r = yr[:, t % 2, :]
                    link(dve.scalar_tensor_tensor(r, r, nmu[:, TILES + t:TILES + t + 1], lnG[:], ALU.add, ALU.mult))
                    dve.wait_ge(rstd_done, TILES + t + 1)
                    for w in [slice(0, D)] if t < TILES - 1 else [slice(0, 512), slice(512, D)]:
                        dve.scalar_tensor_tensor(r[:, w], r[:, w], rstd[:, TILES + t:TILES + t + 1], lnB[:, w], ALU.mult, ALU.add).then_inc(yb_done, 1)
                for i in SLOTS.get(NU + m, []):
                    slot(i)

        @block.gpsimd
        def _(pool):
            steps = [0]

            def link(ins):
                steps[0] += 1
                ins.then_inc(pool_step, 1)
                pool.wait_ge(pool_step, steps[0])

            def inv_std(t):
                pool.wait_ge(stats_done, t + 1)
                power = pool.tensor_tensor(rstd[:, t:t + 1], veps[:, t:t + 1], mhalf[:], ALU.pow)
                if t < TILES:
                    link(power)
                    power = pool.tensor_tensor(nmr[:, t:t + 1], nmu[:, t:t + 1], rstd[:, t:t + 1], ALU.mult)
                power.then_inc(rstd_done, 1)

            def w_low(b):
                pool.wait_ge(whi_done, b + 1)
                pool.tensor_tensor(w_lo[:, b % 2], w_raw[:, b % RAW], w_hi[:, b % 2].bitcast(F32), ALU.subtract).then_inc(wlo_done, 1)

            def h_low(c, groups):
                for g in groups:
                    pool.wait_ge(hhi_done, H_ORDER.index((c, g)) + 1)
                    w = slice(2 * g, 2 * g + 2)
                    pool.tensor_tensor(h_lo[:, w, cols(c)], xnT[:, w, cols(c)], h_hi[:, w, cols(c)].bitcast(F32), ALU.subtract).then_inc(hlo_p, 1)

            def window_sums(s, part):
                g = GROUPS[s]
                if s == 0 and part == 0:
                    pool.wait_ge(rope_done, 15)
                    link(pool.memset(uext[:, 0:HIST], 0.0))
                pool.wait_ge(act_free, freed_count(unit_index("u", g, 1 + part))[1])
                if part:
                    pool.wait_ge(ld_hist, 16 * (s + 1))
                elif s:
                    pool.wait_ge(unit_done, unit_index("z", GROUPS[s - 1], NCH - 1) + 1)
                src, lag = uext, 1
                for m in range(g + 1):
                    dst = sA if m % 2 == 0 else sB
                    end = HIST + 2 * CW - (lag - 1)
                    a, b = (end, UW) if part else (2 * lag - 1, end)
                    ins = pool.tensor_tensor(dst[:, a:b], src[:, a:b], src[:, a - lag:b - lag], ALU.add)
                    if m < g or not part:
                        link(ins)
                    src, lag = dst, 2 * lag
                if part:
                    ins.then_inc(sum_done, 1)

            pool.wait_ge(consts_v, 1)
            inv_std(0)
            inv_std(1)
            inv_std(2)
            h_low(0, (0,))
            inv_std(3)
            inv_std(4)
            inv_std(5)
            inv_std(6)
            inv_std(7)
            inv_std(8)
            h_low(0, (2,))
            h_low(1, (2,))
            h_low(2, (0, 2))
            for b in range(2, NBLK):
                s = (b - 12) // 2 if b < NBLK - 1 else 3
                if b >= 12 and (b % 2 == 0):
                    window_sums(s, 0)
                w_low(b)
                if b >= 12 and (b % 2 == 0):
                    window_sums(s, 1)
            window_sums(3, 0)
            window_sums(3, 1)
            for k in POOL_WO:
                pool.wait_ge(whi_done, NBLK + k + 1)
                pool.tensor_tensor(wo_lo[:, k, :], w_out_raw(k), wo_hi[:, k, :].bitcast(F32), ALU.subtract).then_inc(wlo_done, 1)
            for t in range(TILES):
                if t + 1 < TILES:
                    pool.wait_ge(mhi_done, t + 2)
                    pool.tensor_tensor(m_lo[:, (t + 1) % 2], mixed[:, :, P * (t + 1):P * (t + 2)], m_hi[:, (t + 1) % 2].bitcast(F32),
                                       ALU.subtract).then_inc(mlo_p, 1)
                inv_std(TILES + t)



def head_dims():
    return np.concatenate([np.r_[16 * q:16 * q + 16, 32 + 16 * q:32 + 16 * q + 16] for q in range(2)])


def projection_columns():
    perm = head_dims()
    pair = [np.r_[HD * j:HD * (j + 1), HD * (4 + j):HD * (5 + j)] for j in range(4)]
    qpair = [np.r_[HD * j + perm, HD * (4 + j) + perm] for j in range(4)]
    k = 512 + np.r_[perm, HD + perm]
    v = 640 + np.arange(P)
    ga = [768 + p for p in pair]
    pooled = [a for g in GROUPS for a in (1280 + P * g + np.arange(P), 1792 + P * g + np.arange(P))]
    return np.concatenate([k, v, *ga, *qpair, *pooled])


def tables():
    pos = np.concatenate([np.arange(SEQ), np.tile(1024 + np.arange(LS), NSEQ)]).astype(np.float32)
    half = HD // 2
    inv = (10000.0 ** (-np.arange(half) / half)).astype(np.float32)
    ang = (inv[:, None] * pos[None, :]).astype(np.float64)
    perm = head_dims()
    rows = np.r_[perm, perm]
    cos = np.cos(ang).astype(np.float32)[rows % half]
    sin = np.sin(ang).astype(np.float32)[rows % half] * np.where(rows < half, -1.0, 1.0).astype(np.float32)[:, None]
    ident = np.eye(P, dtype=np.float32)
    sel = np.zeros((P, 9), np.float32)
    ebc = np.zeros((P, 2, P), np.float32)
    for g in range(4):
        for s in range(9):
            sel[32 * g + s, s] = 1.0
        ebc[32 * g, 0, :] = 1.0
        for s in range(NSEQ):
            ebc[32 * g + 1 + s, 1, LS * s:LS * (s + 1)] = 1.0
    ebc[9, :, :] = 1.0
    return cos, np.ascontiguousarray(sin), ident, sel, ebc


def kernel(x_prompt, x_sample, cache_k, cache_v, state_pool, c_prompt, c_sample, w_ada, b_ada, w_in, attn_sinks, w_pool,
           pool_scale, w_out, ln_g, ln_b):
    import concourse.bacc as bacc
    from concourse.bass_utils import run_bass_kernel_spmd

    A = np.asarray
    cos, sin, ident, sel, ebc = tables()
    perm = head_dims()
    c_all = np.concatenate([A(c_prompt), A(c_sample)], 0)
    sinks = A(attn_sinks)[0]
    kc = A(cache_k)[0][..., perm].reshape(NSEQ, WIN, P)
    vcn = A(cache_v)[0].reshape(NSEQ, WIN, P)
    pair = np.concatenate([np.r_[HD * j:HD * (j + 1), HD * (4 + j):HD * (5 + j)] for j in range(4)])
    arrays = {
        "x_all": np.concatenate([A(x_prompt)[0], A(x_sample).reshape(-1, D)], 0).reshape(TILES, P, D),
        "cT_d": c_all.T.reshape(KT, P, 9).transpose(1, 0, 2),
        "bT_d": A(b_ada)[0].reshape(24, P).T,
        "w_ada": A(w_ada)[0].reshape(KT, P, 6, 512).transpose(2, 1, 0, 3),
        "w_in": A(w_in)[0][:, projection_columns()].reshape(KT, P, NBLK, P).transpose(2, 1, 0, 3),
        "w_out": A(w_out)[0][np.r_[pair, 512:1024]].reshape(KT, P, D),
        "w_pool": A(w_pool)[0].transpose(1, 0, 2),
        "pscale_d": A(pool_scale)[0].reshape(4, P).T,
        "sinkp_d": np.repeat(sinks.reshape(4, 2).T, QB, axis=0),
        "sinks_d": np.tile(np.repeat(sinks.reshape(2, 4).T, LS, axis=0), (2, 1)),
        "kcT": kc.transpose(0, 2, 1),
        "vc": vcn,
        "kc_tail": kc[:, LS:, :],
        "vc_tail": vcn[:, LS:, :],
        "histT": A(state_pool)[0].reshape(NSEQ, HIST, 4, P).transpose(2, 3, 0, 1),
        "ln_g": A(ln_g).reshape(1, D),
        "ln_b": A(ln_b).reshape(1, D),
        "ident_d": ident, "sel_d": sel, "ebc_d": ebc,
        "brow_d": A(b_ada)[0][2 * D:].reshape(1, 2, 512),
        "cos_d": cos, "sin_d": sin,
    }
    outs = {
        "y_out": (TILES, P, D), "kT_out": (P, 2 * WIN), "vT_out": (P, 2 * WIN), "upT_out": (4, P, HIST),
        "usT_out": (4, P, NSEQ, HIST), "kcT_out": (NSEQ, WIN - LS, P), "vc_out": (NSEQ, WIN - LS, P),
    }
    nc = bacc.Bacc("TRN2", target_bir_lowering=False, num_devices=1, dynamic_dma_scratch_size=1024)
    arrays = {n: np.ascontiguousarray(a) for n, a in arrays.items()}
    args = {n: nc.dram_tensor(n, a.shape, mybir.dt.from_np(a.dtype), kind="ExternalInput").ap() for n, a in arrays.items()}
    args.update({n: nc.dram_tensor(n, s, F32, kind="ExternalOutput").ap() for n, s in outs.items()})
    hybrid_step(nc, **args)
    r = run_bass_kernel_spmd(nc, [arrays], core_ids=[0]).results[0]

    inv = np.argsort(perm)
    y = r["y_out"].reshape(TOK, D)
    kn = r["kT_out"].T.reshape(2 * WIN, 2, HD)[..., inv]
    vn = r["vT_out"].T.reshape(2 * WIN, 2, HD)

    def sample_cache(old, new):
        return np.concatenate([old.reshape(NSEQ, WIN - LS, 2, HD), new[WIN:].reshape(NSEQ, LS, 2, HD)], 1)[None]

    up = r["upT_out"].transpose(2, 0, 1).reshape(1, 1, HIST, 512)
    us = r["usT_out"].transpose(2, 3, 0, 1).reshape(1, NSEQ, HIST, 512)
    return (y[:SEQ].reshape(1, SEQ, D), y[SEQ:].reshape(NSEQ, LS, D), kn[None, None, :WIN], vn[None, None, :WIN], up,
            sample_cache(r["kcT_out"].reshape(NSEQ, WIN - LS, 2, HD)[..., inv], kn), sample_cache(r["vc_out"], vn), us)
```
